# Optimizing a Trainium2 kernel written in Bass

```python
import numpy as np
import jax, jax.numpy as jnp
from jax import lax

D_MODEL = 1024
BATCH = 1
SEQ = 512
DEPTH = 2

D_MIX = D_MODEL
D_LRU = D_MIX // 2
H_LRU = 8
LRU_BLK = D_LRU // H_LRU
CONV_W = 4
LRU_C = 8.0
D_NSA = D_MIX - D_LRU
HEAD_DIM = 64
N_HEADS = D_NSA // HEAD_DIM
N_KV = 2
GROUP = N_HEADS // N_KV
KV_W = N_KV * HEAD_DIM
CMP_LEN = 32
CMP_STRIDE = 16
CMP_HID = 256
SLC_BLK = 64
SLC_TOPK = 16
WINDOW = 512
WIN_QBLK = 128
SLC_QBLK = 64
ROPE_THETA = 10000.0
EPS = 1e-6
NEG = -1e30
FORCE_BONUS = 1e4
SCALE = HEAD_DIM ** -0.5
D_IN = 2 * D_LRU + 2 * D_NSA + 6 * KV_W + 3 * N_HEADS

kernel_name = 'hymba_griffin_nsa_hybrid'

F32 = jnp.float32

def rmsnorm(x, g):
    xf = x.astype(F32)
    y = xf * lax.rsqrt(jnp.mean(xf * xf, axis=-1, keepdims=True) + EPS)
    return (y * g.astype(F32)).astype(x.dtype)

def rope_tables(seq):
    inv = 1.0 / (ROPE_THETA ** (jnp.arange(0, HEAD_DIM, 2, dtype=F32) / HEAD_DIM))
    ang = jnp.arange(seq, dtype=F32)[:, None] * inv[None, :]
    return jnp.cos(ang), jnp.sin(ang)

def apply_rope(t, cos, sin):
    x1, x2 = jnp.split(t.astype(F32), 2, axis=-1)
    c = cos[None, :, None, :]
    s = sin[None, :, None, :]
    return jnp.concatenate([x1 * c - x2 * s, x2 * c + x1 * s], axis=-1).astype(t.dtype)

def causal_depthwise_conv(u, w, b):
    out = lax.conv_general_dilated(u, w[:, None, :].astype(u.dtype), window_strides=(1,), padding=[(CONV_W - 1, 0)], dimension_numbers=('NWC', 'WIO', 'NWC'), feature_group_count=u.shape[-1])
    return out + b

def rg_lru(u, wa, ba, wi, bi, lam):
    B, S, _ = u.shape
    uf = u.astype(F32)
    uh = uf.reshape(B, S, H_LRU, LRU_BLK)
    r = jax.nn.sigmoid(jnp.einsum('bshi,hij->bshj', uh, wa.astype(F32)).reshape(B, S, D_LRU) + ba.astype(F32))
    i = jax.nn.sigmoid(jnp.einsum('bshi,hij->bshj', uh, wi.astype(F32)).reshape(B, S, D_LRU) + bi.astype(F32))
    log_a = -LRU_C * r * jax.nn.softplus(-lam.astype(F32))
    a = jnp.exp(log_a)
    drive = jnp.sqrt(-jnp.expm1(2.0 * log_a)) * (i * uf)

    def combine(lhs, rhs):
        a1, b1 = lhs
        a2, b2 = rhs
        return a1 * a2, a2 * b1 + b2

    _, h = lax.associative_scan(combine, (a, drive), axis=1)
    return h

def compress(kv, pos, w1, w2):
    B, S, Hk, dh = kv.shape
    n_sub = S // CMP_STRIDE
    ratio = CMP_LEN // CMP_STRIDE
    nc = n_sub - ratio + 1
    sub = kv.reshape(B, n_sub, CMP_STRIDE, Hk, dh)
    blocks = jnp.concatenate([sub[:, r:r + nc] for r in range(ratio)], axis=2)
    blocks = blocks + pos[None, None, :, None, :]
    flat = jnp.moveaxis(blocks, 3, 2).reshape(B, nc, Hk, CMP_LEN * dh)
    return jax.nn.silu(flat @ w1) @ w2

def cmp_attention(q, kc, vc):
    B, S, H, dh = q.shape
    nc = kc.shape[1]
    qg = q.reshape(B, S, N_KV, GROUP, dh)
    s = jnp.einsum('bskgd,bckd->bkgsc', qg, kc, preferred_element_type=F32) * SCALE
    t = jnp.arange(S)
    blk_end = jnp.arange(nc) * CMP_STRIDE + CMP_LEN - 1
    valid = blk_end[None, :] <= t[:, None]
    s = jnp.where(valid, s, NEG)
    p = jnp.where(valid, jax.nn.softmax(s, axis=-1), 0.0)
    o = jnp.einsum('bkgsc,bckd->bskgd', p, vc.astype(F32)).reshape(B, S, H, dh)
    return o, p

def selection_indices(p_cmp, seq):
    nc = p_cmp.shape[-1]
    n_slc = seq // SLC_BLK
    c0 = np.arange(nc)[:, None] * CMP_STRIDE
    j0 = np.arange(n_slc)[None, :] * SLC_BLK
    overlap = np.clip(np.minimum(c0 + CMP_LEN, j0 + SLC_BLK) - np.maximum(c0, j0), 0, None) / CMP_LEN
    m = jnp.asarray(overlap, dtype=F32)
    p_slc = jnp.einsum('bkgsc,cj->bksj', p_cmp, m)
    cur = (jnp.arange(seq) // SLC_BLK)[:, None]
    jj = jnp.arange(n_slc)[None, :]
    forced = (jj == 0) | (jj == cur) | (jj == cur - 1)
    score = jnp.where(forced, p_slc + FORCE_BONUS, p_slc)
    score = jnp.where(jj <= cur, score, NEG)
    k = min(SLC_TOPK, n_slc)
    top_s, idx = lax.top_k(score, k)
    return idx, top_s > NEG / 2

def slc_attention(q, k, v, idx, ok):
    B, S, H, dh = q.shape
    n_slc = S // SLC_BLK
    kk = idx.shape[-1]
    nq = S // SLC_QBLK
    kb = jnp.moveaxis(k.reshape(B, n_slc, SLC_BLK, N_KV, dh), 3, 1)
    vb = jnp.moveaxis(v.reshape(B, n_slc, SLC_BLK, N_KV, dh), 3, 1)
    qc = jnp.moveaxis(q.reshape(B, nq, SLC_QBLK, N_KV, GROUP, dh), 1, 0)
    ic = jnp.moveaxis(idx.reshape(B, N_KV, nq, SLC_QBLK, kk), 2, 0)
    okc = jnp.moveaxis(ok.reshape(B, N_KV, nq, SLC_QBLK, kk), 2, 0)
    tc = jnp.arange(S).reshape(nq, SLC_QBLK)
    gather = jax.vmap(jax.vmap(lambda blocks, ix: blocks[ix]))

    def one_block(args):
        qb, ib, okb, tb = args
        ks = gather(kb, ib)
        vs = gather(vb, ib)
        s = jnp.einsum('bqkgd,bkqnpd->bkgqnp', qb, ks, preferred_element_type=F32) * SCALE
        tok = ib[..., None] * SLC_BLK + jnp.arange(SLC_BLK)
        mask = okb[..., None] & (tok <= tb[None, None, :, None, None])
        s = jnp.where(mask[:, :, None], s, NEG)
        p = jax.nn.softmax(s.reshape(B, N_KV, GROUP, SLC_QBLK, kk * SLC_BLK), axis=-1).reshape(s.shape)
        return jnp.einsum('bkgqnp,bkqnpd->bqkgd', p, vs.astype(F32))

    out = lax.map(one_block, (qc, ic, okc, tc))
    return jnp.moveaxis(out, 0, 1).reshape(B, S, H, dh)

def win_attention(q, k, v):
    B, S, H, dh = q.shape
    nb = S // WIN_QBLK
    nback = WINDOW // WIN_QBLK
    pad = ((0, 0), (WINDOW, 0), (0, 0), (0, 0))
    kp = jnp.pad(k, pad).reshape(B, nb + nback, WIN_QBLK, N_KV, dh)
    vp = jnp.pad(v, pad).reshape(B, nb + nback, WIN_QBLK, N_KV, dh)
    kw = jnp.concatenate([kp[:, j:j + nb] for j in range(nback + 1)], axis=2)
    vw = jnp.concatenate([vp[:, j:j + nb] for j in range(nback + 1)], axis=2)
    qb = q.reshape(B, nb, WIN_QBLK, N_KV, GROUP, dh)
    s = jnp.einsum('bnqkgd,bnpkd->bnkgqp', qb, kw, preferred_element_type=F32) * SCALE
    n_idx = jnp.arange(nb)[:, None]
    tq = n_idx * WIN_QBLK + jnp.arange(WIN_QBLK)[None, :]
    tk = n_idx * WIN_QBLK - WINDOW + jnp.arange((nback + 1) * WIN_QBLK)[None, :]
    diff = tq[:, :, None] - tk[:, None, :]
    mask = (diff >= 0) & (diff < WINDOW) & (tk[:, None, :] >= 0)
    s = jnp.where(mask[None, :, None, None], s, NEG)
    p = jax.nn.softmax(s, axis=-1)
    return jnp.einsum('bnkgqp,bnpkd->bnqkgd', p, vw.astype(F32)).reshape(B, S, H, dh)

def hybrid_layer(x, g, w_in, conv_w, conv_b, wa, ba, wi, bi, lam, pos_k, pos_v, kw1, kw2, vw1, vw2, w_out, cos, sin):
    B, S, _ = x.shape
    h = rmsnorm(x, g)
    z = h @ w_in
    splits = [int(c) for c in np.cumsum([D_LRU, D_LRU, D_NSA, D_NSA, KV_W, KV_W, KV_W, KV_W, KV_W, KV_W])]
    u_lru, g_lru, q, g_nsa, kc, vc, ks, vs, kwn, vwn, gate_logits = jnp.split(z, splits, axis=-1)
    y_lru = rg_lru(causal_depthwise_conv(u_lru, conv_w, conv_b), wa, ba, wi, bi, lam)
    heads = lambda t: t.reshape(B, S, N_KV, HEAD_DIM)
    q = q.reshape(B, S, N_HEADS, HEAD_DIM)
    o_cmp, p_cmp = cmp_attention(q, compress(heads(kc), pos_k, kw1, kw2), compress(heads(vc), pos_v, vw1, vw2))
    idx, ok = selection_indices(p_cmp, S)
    q_rot = apply_rope(q, cos, sin)
    o_slc = slc_attention(q_rot, apply_rope(heads(ks), cos, sin), heads(vs), idx, ok)
    o_win = win_attention(q_rot, apply_rope(heads(kwn), cos, sin), heads(vwn))
    gates = jax.nn.sigmoid(gate_logits.astype(F32)).reshape(B, S, N_HEADS, 3)
    y_nsa = (gates[..., 0:1] * o_cmp + gates[..., 1:2] * o_slc + gates[..., 2:3] * o_win).reshape(B, S, D_NSA)
    y = jnp.concatenate([y_lru * jax.nn.silu(g_lru.astype(F32)), y_nsa * jax.nn.silu(g_nsa.astype(F32))], axis=-1).astype(x.dtype)
    return x + y @ w_out

def setup_inputs(seed: int = 0) -> dict:
    key = jax.random.key(seed)
    ks = jax.random.split(key, 20)
    nrm = lambda k, shape, scale: jax.random.normal(k, shape, dtype=F32) * scale
    u = jax.random.uniform(ks[7], (DEPTH, D_LRU), dtype=F32, minval=0.9, maxval=0.999)
    a0 = u ** (1.0 / LRU_C)
    return {
        'x': nrm(ks[0], (BATCH, SEQ, D_MODEL), 1.0),
        'norm_g': 1.0 + nrm(ks[1], (DEPTH, D_MODEL), 0.02),
        'w_in': nrm(ks[2], (DEPTH, D_MODEL, D_IN), D_MODEL ** -0.5),
        'conv_w': nrm(ks[3], (DEPTH, CONV_W, D_LRU), CONV_W ** -0.5),
        'conv_b': nrm(ks[4], (DEPTH, D_LRU), 0.02),
        'lru_wa': nrm(ks[5], (DEPTH, H_LRU, LRU_BLK, LRU_BLK), LRU_BLK ** -0.5),
        'lru_ba': nrm(ks[6], (DEPTH, D_LRU), 0.02),
        'lru_wi': nrm(ks[8], (DEPTH, H_LRU, LRU_BLK, LRU_BLK), LRU_BLK ** -0.5),
        'lru_bi': nrm(ks[9], (DEPTH, D_LRU), 0.02),
        'lru_lambda': jnp.log(a0) - jnp.log1p(-a0),
        'cmp_pos_k': nrm(ks[10], (DEPTH, CMP_LEN, HEAD_DIM), 0.1),
        'cmp_pos_v': nrm(ks[11], (DEPTH, CMP_LEN, HEAD_DIM), 0.1),
        'cmp_k_w1': nrm(ks[12], (DEPTH, CMP_LEN * HEAD_DIM, CMP_HID), (CMP_LEN * HEAD_DIM) ** -0.5),
        'cmp_k_w2': nrm(ks[13], (DEPTH, CMP_HID, HEAD_DIM), CMP_HID ** -0.5),
        'cmp_v_w1': nrm(ks[14], (DEPTH, CMP_LEN * HEAD_DIM, CMP_HID), (CMP_LEN * HEAD_DIM) ** -0.5),
        'cmp_v_w2': nrm(ks[15], (DEPTH, CMP_HID, HEAD_DIM), CMP_HID ** -0.5),
        'w_out': nrm(ks[16], (DEPTH, D_MIX, D_MODEL), D_MIX ** -0.5),
        'final_g': 1.0 + nrm(ks[17], (D_MODEL,), 0.02),
    }

def reference(x, norm_g, w_in, conv_w, conv_b, lru_wa, lru_ba, lru_wi, lru_bi, lru_lambda, cmp_pos_k, cmp_pos_v, cmp_k_w1, cmp_k_w2, cmp_v_w1, cmp_v_w2, w_out, final_g):
    cos, sin = rope_tables(x.shape[1])
    h = x
    for l in range(DEPTH):
        h = hybrid_layer(h, norm_g[l], w_in[l], conv_w[l], conv_b[l], lru_wa[l], lru_ba[l], lru_wi[l], lru_bi[l], lru_lambda[l], cmp_pos_k[l], cmp_pos_v[l], cmp_k_w1[l], cmp_k_w2[l], cmp_v_w1[l], cmp_v_w2[l], w_out[l], cos, sin)
    return rmsnorm(h, final_g)


_drawn_inputs = setup_inputs


def setup_inputs(seed=0):
    import zlib

    import numpy as np

    out = dict(_drawn_inputs(seed))
    spreads = {}
    factors = {'norm_g': 4.944,
     'lru_ba': 8.0,
     'lru_bi': 8.0,
     'cmp_pos_k': 8.0,
     'cmp_pos_v': 3.366,
     'final_g': 2.875}
    for name, (base, spread) in spreads.items():
        noise = np.random.default_rng([zlib.crc32(name.encode()), seed]).standard_normal(out[name].shape)
        drawn = base * np.exp(spread * noise) if base else spread * noise
        out[name] = __import__('jax').numpy.asarray(drawn.astype(out[name].dtype))
    for name, factor in factors.items():
        out[name] = (out[name] * factor).astype(out[name].dtype)
    return out
```

```python
from contextlib import ExitStack

import numpy as np

import concourse.bass as bass
from concourse import mybir

F32, F32R, BF16 = mybir.dt.float32, mybir.dt.float32r, mybir.dt.bfloat16
ALU, ACT, AX = mybir.AluOpType, mybir.ActivationFunctionType, mybir.AxisListType

P = 128
D_MODEL, SEQ, DEPTH = 1024, 512, 2
D_LRU = D_NSA = 512
LRU_BLK, CONV_W = 64, 4
HD, N_KV, GROUP = 64, 2, 4
CMP_LEN, CMP_STRIDE, CMP_HID = 32, 16, 256
EPS, BIG = 1e-6, 1e30
KT = D_MODEL // P
TT = SEQ // P
CT = D_LRU // P
NC = SEQ // CMP_STRIDE - CMP_LEN // CMP_STRIDE + 1
NPAIR = CMP_LEN // 2
NCOL = N_KV * NC + 1
HT = CMP_HID // P
COL_U, COL_GL, COL_Q, COL_GN = 0, 512, 1024, 1536
COL_KC, COL_VC, COL_KS, COL_VS, COL_KW, COL_VW, COL_GATE = 2048, 2176, 2304, 2432, 2560, 2688, 2816
N_GATE = 24
PG, PFG, PCW, PCB, PBA, PBI, PLAM, NPAR = 0, 16, 24, 56, 64, 72, 80, 88
N_STAGE, N_RING, N_PT = 2, 2, 4
FILL = {(3, 0): ("gn0", "gn1"), (3, 1): ("gn2", "gn3")}


def schedule():
    s = []
    for l in range(DEPTH):
        s += [("Z", l, f"gl{t}") for t in range(CT)]
        s += [("Z", l, "u0"), ("Z", l, "u1"), ("GATES", l, 0), ("Z", l, "kc"), ("GATES", l, 1), ("Z", l, "vc"),
              ("LRU", l, 0), ("Z", l, "u2"), ("CMP", l, 0), ("Z", l, "u3"), ("GATES", l, 2), ("CMP", l, 1),
              ("Z", l, "ks"), ("GATES", l, 3), ("Z", l, "kw"), ("LRU", l, 1), ("ROPE", l, "ks"), ("Z", l, "vs"),
              ("ROPE", l, "kw"), ("Z", l, "vw"), ("TURN", l, "vs"), ("Z", l, "gate"), ("TURN", l, "vw"),
              ("Z", l, "q0"), ("TURN", l, "gate"), ("Z", l, "q1"), ("ROPE", l, "q0"), ("Z", l, "q2"),
              ("ROPE", l, "q1"), ("Z", l, "q3"), ("ROPE", l, "q2"), ("ROPE", l, "q3"), ("CSOFT", l)]
        for i in reversed(range(TT)):
            for b in range(2):
                s.append(("UNIT", l, i, b, FILL.get((i, b), ())))
        s += [("OUT", l, m) for m in range(KT)]
        s.append(("NORM", l))
    s.append(("FINAL",))
    return s


def stem(name):
    return name.rstrip("0123")


class Plan:

    def __init__(self, sched):
        self.split = []
        self.z = [(("X", m), "act") for m in range(KT)]
        self.aux = [("params", "dve"), ("pos", "dve"), (("ss", -1), "dve"), (("rb", -1), "act")]
        self.e = []
        for st in sched:
            k = st[0]
            if k in ("Z", "OUT"):
                self.chunk(st)
                if k == "Z" and stem(st[2]) != "u":
                    self.e.append(st[1:])
            elif k == "GATES":
                self.z += [((*st, "a"), "act"), ((*st, "i"), "act")]
            elif k == "CMP":
                self.aux += [((*st, 1), "dve"), ((*st, 2), "dve")]
            elif k == "TURN":
                self.aux.append((st, "act"))
            elif k == "ROPE" and stem(st[2]) == "q":
                self.aux.append((st, "dve"))
            elif k == "UNIT":
                for name in st[4]:
                    self.chunk(("Z", st[1], name))
                    self.e.append((st[1], name))
                if st[3] == 1:
                    self.e.append((st[1], f"y{st[2]}"))
            elif k == "NORM":
                self.aux += [(("ss", st[1]), "dve"), (("rb", st[1]), "act")]
            elif k == "FINAL":
                self.z += [(("F", m), "tok") for m in range(KT)]
        self.loads, n = self.split[:N_RING], N_RING
        for st in sched:
            if st[0] == "CMP":
                self.loads += [(*st, c) for c in range(4)]
            steps = self.steps_ahead(st)
            self.loads += self.split[n:n + steps]
            n += steps
        self.split_no = {key: n for n, key in enumerate(self.split)}
        self.load_no = {key: n for n, key in enumerate(self.loads)}
        self.z_no = {key: n for n, (key, _) in enumerate(self.z)}
        self.aux_no = {key: n for n, (key, _) in enumerate(self.aux)}
        self.e_no = {key: n for n, key in enumerate(self.e)}
        self.rope = [st[1:] for st in sched if st[0] == "ROPE"]
        self.rope_no = {key: n for n, key in enumerate(self.rope)}
        self.units = [st[1:4] for st in sched if st[0] == "UNIT"]
        self.unit_no = {key: n for n, key in enumerate(self.units)}
        self.turns, self.first_turn = 0, {}
        for key in self.units:
            self.first_turn[key] = self.turns
            self.turns += self.turns_of(key)
        self.staged_at, count = {}, [0] * N_STAGE
        for n, key in enumerate(self.loads):
            count[n % N_STAGE] += 16 * self.pieces(key)
            self.staged_at[key] = count[n % N_STAGE]
        self.stacked_at, n = [], 0
        for _, name in self.rope:
            n += 64 if stem(name) == "q" else 128
            self.stacked_at.append(n)

    def chunk(self, st):
        self.split.append(st)
        self.z.append((st, "out" if st[0] == "OUT" else "dve"))

    @staticmethod
    def steps_ahead(st):
        return 1 if st[0] in ("Z", "OUT") else len(st[4]) if st[0] == "UNIT" else 0

    @staticmethod
    def turns_of(key):
        _, i, b = key
        return i + 1 + (b == 1)

    @staticmethod
    def pieces(key):
        if key[0] == "OUT":
            return 3
        return 2 if key[0] == "Z" and stem(key[2]) in ("q", "gn", "gate") else 1

    def freed(self, uses, n):
        who = uses[n][1]
        return who, sum(w == who for _, w in uses[:n + 1])


def hybrid_trunk(nc, x, norm_g, w_in, conv_w, conv_b, lru_wa, lru_ba, lru_wi, lru_bi, lru_lambda,
                 cmp_pos_k, cmp_pos_v, cmp_k_w1, cmp_k_w2, cmp_v_w1, cmp_v_w2, w_out, final_g,
                 rope_cos, rope_sin, out):
    sched = schedule()
    plan = Plan(sched)
    split_no, load_no, z_no, aux_no, e_no = plan.split_no, plan.load_no, plan.z_no, plan.aux_no, plan.e_no
    rope_no, unit_no, first_turn = plan.rope_no, plan.unit_no, plan.first_turn

    ctx = ExitStack()
    with ctx:
        def sb(name, shape, dt=F32):
            return ctx.enter_context(nc.sbuf_tensor(name, shape, dt))

        def sem(name):
            return ctx.enter_context(nc.semaphore(name))

        def psum(name, n):
            return [ctx.enter_context(nc.psum_tensor(f"{name}{k}", [P, SEQ], F32)) for k in range(n)]

        xT = sb("xT", [P, KT, SEQ])
        h_hi, h_lo = sb("h_hi", [P, KT, SEQ], F32R), sb("h_lo", [P, KT, SEQ], F32R)
        y_hi, y_lo = sb("y_hi", [P, KT, SEQ], F32R), sb("y_lo", [P, KT, SEQ], F32R)
        stage = sb("stage", [P, N_STAGE, KT * P])
        w_hi, w_lo = sb("w_hi", [P, N_RING, KT * P], F32R), sb("w_lo", [P, N_RING, KT * P], F32R)
        probs = sb("probs", [P, 8, SEQ])
        probsT = sb("probsT", [P, N_PT, SEQ])
        q_st = sb("q_st", [P, 8, SEQ], F32R)
        k_st = sb("k_st", [P, 2, N_KV, 2, SEQ], F32R)
        v_sb = sb("v_sb", [P, 2, TT, P])
        silu_g = sb("silu_g", [P, 4, SEQ])
        cosT, sinT = sb("cosT", [P, SEQ]), sb("sinT", [P, SEQ])
        ident, ones = sb("ident", [P, P]), sb("ones", [P, P])
        ident_b, causal_b = sb("ident_b", [P, P], BF16), sb("causal_b", [P, P], BF16)
        E = sb("E", [P, 2, SEQ])
        swp = sb("swp", [P, SEQ])
        r_hi, r_lo = sb("r_hi", [P, SEQ], F32R), sb("r_lo", [P, SEQ], F32R)
        rstd = sb("rstd", [P, SEQ])
        upad = sb("upad", [P, SEQ + CONV_W - 1])
        cmpb = sb("cmpb", [P, NPAIR * NCOL])
        bd = sb("bd", [P, CT, 2, P])
        w2 = sb("w2", [P, 2, HT, HD])
        par, posT = sb("par", [P, NPAR]), sb("posT", [P, 2, DEPTH, NPAIR])
        hb, hid = sb("hb", [P, HT, NCOL]), sb("hid", [P, HT, NCOL - 1])
        kc_bd, vc_sb = sb("kc_bd", [P, N_KV * NC]), sb("vc_sb", [NC, N_KV, HD])
        mask_c, row_ok = sb("mask_c", [P, TT, NC]), sb("row_ok", [P, TT])
        gates = sb("gates", [P, TT, N_GATE])
        mn, rs, coef = sb("mn", [P, 2, 8]), sb("rs", [P, 2, 8]), sb("coef", [P, 2, 8])
        mnc, rsc = sb("mnc", [P, TT, 8]), sb("rsc", [P, TT, 8])
        soft = sb("soft", [P, 5, 8])
        nsp, psp = sb("nsp", [P, 8]), sb("psp", [P, 8])
        hba, hbi = sb("hba", [P, 8]), sb("hbi", [P, 8])
        ms, mhalf, rt = sb("ms", [P, TT]), sb("mhalf", [P, TT]), sb("rt", [P, TT])

        par_row, pos_row = E[:, 0, 0:P], E[:, 0, P:2 * P]
        flat = cmpb[:, :].rearrange("p (j c) -> p j c", c=NCOL)
        sc = cmpb[:, 0:TT * 8 * NC].rearrange("p (i h c) -> p i h c", i=TT, c=NC)
        x_tok = probs[:, :, :].rearrange("p (t a) n -> p t (a n)", t=TT)
        sq_tmp, sq_acc = swp, upad[:, CONV_W - 1:]
        diag = probs[:, 0, :]
        UC, A = [probs[:, 0, :], probs[:, 1, :]], [probs[:, 2, :], probs[:, 3, :]]
        M, IU = [probs[:, 4, :], probs[:, 5, :]], [probs[:, 6, :], probs[:, 7, :]]
        THR, THI, TH, SQ = (probsT[:, n, :] for n in range(4))

        z_ps, s_ps, t_ps = psum("z_ps", 2), psum("s_ps", 2), psum("t_ps", 2)
        (o_ps,), (a_ps,) = psum("o_ps", 1), psum("a_ps", 1)

        x_in, par_in, tab_in, small_in = sem("x_in"), sem("par_in"), sem("tab_in"), sem("small_in")
        staged = [sem(f"staged{k}") for k in range(N_STAGE)]
        swapped, stacked, stored = sem("swapped"), sem("stacked"), sem("stored")
        hi_split, lo_split, cmp_used = sem("hi_split"), sem("lo_split"), sem("cmp_used")
        z_full, z_dve, z_act = sem("z_full"), sem("z_dve"), sem("z_act")
        a_full, a_dve, a_act = sem("a_full"), sem("a_dve"), sem("a_act")
        s_full, t_full = sem("s_full"), sem("t_full")
        dve_link, act_link, pool_link = sem("dve_link"), sem("act_link"), sem("pool_link")
        consts, par_ok, lam_ok, exp_lam, lru_par = sem("consts"), sem("par_ok"), sem("lam_ok"), sem("exp_lam"), sem("lru_par")
        x_turned, x_new, h_hi_ok, h_lo_ok = sem("x_turned"), sem("x_new"), sem("h_hi_ok"), sem("h_lo_ok")
        squared, sq_added, root_ok, diag_ok = sem("squared"), sem("sq_added"), sem("root_ok"), sem("diag_ok")
        gate_tanh, silu_ok = sem("gate_tanh"), sem("silu_ok")
        conv_ok, a_ok, th_ok, sq_ok, m_ok, root_m = sem("conv_ok"), sem("a_ok"), sem("th_ok"), sem("sq_ok"), sem("m_ok"), sem("root_m")
        ylru_ok, ylru_hi, ylru_lo = sem("ylru_ok"), sem("ylru_hi"), sem("ylru_lo")
        flat_ok, hid_in, hid_tanh, hid_ok = sem("flat_ok"), sem("hid_in"), sem("hid_tanh"), sem("hid_ok")
        swap_mul, rot_ok, rope_hi, rope_lo = sem("swap_mul"), sem("rot_ok"), sem("rope_hi"), sem("rope_lo")
        cs_sub, cs_exp, cs_ok = sem("cs_sub"), sem("cs_exp"), sem("cs_ok")
        min_ok, exp_ok, p_ok, pt_act, pt_dve, pv_done = sem("min_ok"), sem("exp_ok"), sem("p_ok"), sem("pt_act"), sem("pt_dve"), sem("pv_done")
        ynsa_ok, ynsa_hi, ynsa_lo = sem("ynsa_ok"), sem("ynsa_hi"), sem("ynsa_lo")
        fin_ok, tok_ok = sem("fin_ok"), sem("tok_ok")

        z_free, a_free = {"dve": z_dve, "act": z_act, "out": x_new, "tok": tok_ok}, {"dve": a_dve, "act": a_act}
        N_CONST = 9
        def wait_z(eng, key):
            n = z_no[key]
            if n >= 2:
                who, count = plan.freed(plan.z, n - 2)
                eng.wait_ge(z_free[who], count)

        def wait_aux(eng, key):
            n = aux_no[key]
            if n >= 1:
                who, count = plan.freed(plan.aux, n - 1)
                eng.wait_ge(a_free[who], count)

        def z_bank(key):
            return z_ps[z_no[key] % 2]

        def e_slot(key):
            return E[:, e_no[key] % 2, :]

        def stage_of(key):
            return stage[:, load_no[key] % N_STAGE, :]

        def unit_of_layer(l):
            return 2 * TT * l

        def turns_before(l):
            return plan.turns // DEPTH * l

        def chunk_done(n):
            return z_no[plan.split[n]] + 1

        block = ctx.enter_context(nc.Block())

        @block.sync
        def _(sync):
            for at, src in ((PG, norm_g.rearrange("l (m p) -> (l m) p", p=P)),
                            (PFG, final_g.rearrange("(m p) -> m p", p=P)),
                            (PCW, conv_w.rearrange("l j (t p) -> (l j t) p", p=P)),
                            (PCB, conv_b.rearrange("l (t p) -> (l t) p", p=P)),
                            (PBA, lru_ba.rearrange("l (t p) -> (l t) p", p=P)),
                            (PBI, lru_bi.rearrange("l (t p) -> (l t) p", p=P)),
                            (PLAM, lru_lambda.rearrange("l (t p) -> (l t) p", p=P))):
                sync.dma_start(par_row[at:at + src.shape[0], :], src).then_inc(par_in, 16)
            for kv, pos in enumerate((cmp_pos_k, cmp_pos_v)):
                n = DEPTH * NPAIR
                sync.dma_start(pos_row[kv * n:(kv + 1) * n, :],
                               pos.rearrange("l (j h) d -> (l j) (h d)", h=2)).then_inc(par_in, 16)
            for t in range(TT):
                sync.dma_start(x_tok[:, t, :], x[0, t * P:(t + 1) * P, :]).then_inc(x_in, 16)
            sync.dma_start(cosT[:, :], rope_cos).then_inc(tab_in, 16)
            sync.dma_start(sinT[:, :], rope_sin).then_inc(tab_in, 16)

            def load(n):
                key = plan.loads[n]
                if n >= N_STAGE:
                    old = plan.loads[n - N_STAGE]
                    if old[0] == "CMP":
                        if old[3] == 3:
                            sync.wait_ge(a_full, aux_no[(*old[:3], 1)] + 1)
                        else:
                            sync.wait_ge(cmp_used, 3 * (2 * old[1] + old[2]) + old[3] + 1)
                    else:
                        sync.wait_ge(hi_split, split_no[old] + 1)
                        sync.wait_ge(lo_split, split_no[old] + 1)
                slot, done = stage_of(key), staged[n % N_STAGE]
                if key[0] == "CMP":
                    _, l, kv, c = key
                    w = (cmp_k_w1, cmp_v_w1)[kv][l]
                    sync.dma_start(slot.rearrange("p (j n) -> p j n", j=4),
                                   w[c * 4 * P:(c + 1) * 4 * P, :].rearrange("(j p) n -> p j n", p=P)).then_inc(done, 16)
                    return
                dst = slot.rearrange("p (k n) -> p k n", k=KT)
                if key[0] == "OUT":
                    _, l, m = key
                    cols = w_out[l][:, m * P:(m + 1) * P]
                    sync.dma_start(dst[:, 0:CT, :], cols[0:D_LRU, :].rearrange("(k p) n -> p k n", p=P)).then_inc(done, 16)
                    for g in range(N_KV):
                        sync.dma_start(dst[g * HD:(g + 1) * HD, CT:KT, :],
                                       cols[D_LRU + g * GROUP * HD:D_LRU + (g + 1) * GROUP * HD, :]
                                       .rearrange("(r d) n -> d r n", d=HD)).then_inc(done, 16)
                    return
                _, l, name = key
                w = w_in[l].rearrange("(k p) n -> p k n", p=P)
                if stem(name) in ("q", "gn"):
                    at = (COL_Q if stem(name) == "q" else COL_GN) + int(name[-1]) * HD
                    for g in range(N_KV):
                        src = w[:, :, at + g * GROUP * HD:at + g * GROUP * HD + HD]
                        sync.dma_start(dst[:, :, g * HD:(g + 1) * HD], src).then_inc(done, 16)
                elif name == "gate":
                    sync.dma_start(dst[:, :, 0:N_GATE], w[:, :, COL_GATE:COL_GATE + N_GATE]).then_inc(done, 16)
                    sync.dma_start(dst[:, :, N_GATE:P], w[:, :, COL_GATE - P + N_GATE:COL_GATE]).then_inc(done, 16)
                else:
                    at = {"u": COL_U, "gl": COL_GL, "kc": COL_KC, "vc": COL_VC, "ks": COL_KS, "vs": COL_VS,
                          "kw": COL_KW, "vw": COL_VW}[stem(name)]
                    at += int(name[-1]) * P if name[-1].isdigit() else 0
                    sync.dma_start(dst, w[:, :, at:at + P]).then_inc(done, 16)

            def small_weights(l):
                if l == 0:
                    sync.wait_ge(consts, N_CONST)
                else:
                    sync.wait_ge(z_full, z_no[("GATES", l - 1, CT - 1, "i")] + 1)
                    sync.wait_ge(a_dve, plan.freed(plan.aux, aux_no[("CMP", l - 1, 1, 2)])[1])
                for ab, w in enumerate((lru_wa, lru_wi)):
                    for h in range(2):
                        sync.dma_start(bd[h * HD:(h + 1) * HD, :, ab, h * HD:(h + 1) * HD],
                                       w[l].rearrange("(t h) i j -> h i t j", h=2)[h]).then_inc(small_in, 16)
                for kv, w in enumerate((cmp_k_w2, cmp_v_w2)):
                    sync.dma_start(w2[:, kv, :, :], w[l].rearrange("(m p) d -> p m d", p=P)).then_inc(small_in, 16)

            for n in range(N_STAGE):
                load(n)
            loaded = N_STAGE
            small_weights(0)
            for st in sched:
                kind = st[0]
                if kind == "ROPE":
                    n, (_, l, name) = rope_no[st[1:]], st
                    sync.wait_ge(z_dve, plan.freed(plan.z, z_no[("Z", l, name)])[1])
                    sync.wait_ge(silu_ok, 8 * l + CT)
                    if n >= 1:
                        sync.wait_ge(rot_ok, n)
                    for h in range(4):
                        a, b = 32 * h, 32 * (h ^ 1)
                        sync.dma_start(swp[a:a + 32, :], e_slot(st[1:])[b:b + 32, :]).then_inc(swapped, 16)
                    sync.wait_ge(rope_hi, n + 1)
                    sync.wait_ge(rope_lo, n + 1)
                    if l >= 1 and n == 6 * l:
                        sync.wait_ge(s_full, 8 * unit_of_layer(l))
                    for g in range(N_KV):
                        rows = slice(g * HD, (g + 1) * HD)
                        if stem(name) == "q":
                            head = q_st[:, GROUP * g + int(name[-1]), :]
                            sync.dma_start(head[0:HD, :].bitcast(F32), r_hi[rows, :].bitcast(F32)).then_inc(stacked, 16)
                            sync.dma_start(head[HD:P, :].bitcast(F32), r_lo[rows, :].bitcast(F32)).then_inc(stacked, 16)
                        else:
                            keys = k_st[:, 0 if name == "ks" else 1, g, :, :]
                            sync.dma_start(keys[0:HD, 0, :].bitcast(F32), r_hi[rows, :].bitcast(F32)).then_inc(stacked, 16)
                            sync.dma_start(keys[HD:P, 0, :].bitcast(F32), r_lo[rows, :].bitcast(F32)).then_inc(stacked, 16)
                            sync.dma_start(keys[0:HD, 1, :].bitcast(F32), r_lo[rows, :].bitcast(F32)).then_inc(stacked, 16)
                            sync.dma_start(keys[HD:P, 1, :].bitcast(F32), r_hi[rows, :].bitcast(F32)).then_inc(stacked, 16)
                for _ in range(4 if kind == "CMP" else plan.steps_ahead(st)):
                    if loaded < len(plan.loads):
                        load(loaded)
                        loaded += 1
                if kind == "CSOFT" and st[1] + 1 < DEPTH:
                    small_weights(st[1] + 1)
            for m in range(KT):
                sync.wait_ge(tok_ok, m + 1)
                sync.dma_start(out[0].rearrange("(t p) n -> p t n", p=P)[:, :, m * P:(m + 1) * P],
                               x_tok[:, :, m * P:(m + 1) * P]).then_inc(stored, 16)
            sync.wait_ge(stored, 16 * KT)

        @block.gpsimd
        def _(pool):
            links = [0]

            def link(ins):
                links[0] += 1
                ins.then_inc(pool_link, 1)
                pool.wait_ge(pool_link, links[0])

            pool.memset(bd[:, :, :, :], 0.0).then_inc(consts, 1)
            link(pool.memset(ident[:, :], 0.0))
            link(pool.affine_select(out=ident[:, :], in_=ident[:, :], compare_op=ALU.not_equal, fill=1.0,
                                    base=0, pattern=[[-1, P]], channel_multiplier=1))
            pool.tensor_copy(ident_b[:, :], ident[:, :]).then_inc(consts, 1)
            pool.memset(ones[:, :], 1.0).then_inc(consts, 1)
            link(pool.memset(causal_b[:, :], 0.0))
            pool.affine_select(out=causal_b[:, :], in_=causal_b[:, :], compare_op=ALU.is_ge, fill=BIG, base=0,
                               pattern=[[-1, P]], channel_multiplier=1).then_inc(consts, 1)
            link(pool.memset(mask_c[:, :, :], 0.0))
            pool.affine_select(out=mask_c[:, :, :], in_=mask_c[:, :, :], compare_op=ALU.is_ge, fill=BIG,
                               base=-(CMP_LEN - 1), pattern=[[P, TT], [-CMP_STRIDE, NC]],
                               channel_multiplier=1).then_inc(consts, 1)
            link(pool.memset(row_ok[:, :], 1.0))
            pool.affine_select(out=row_ok[:, :], in_=row_ok[:, :], compare_op=ALU.is_ge, fill=0.0,
                               base=-(CMP_LEN - 1), pattern=[[P, TT]], channel_multiplier=1).then_inc(consts, 1)
            pool.memset(kc_bd[:, :], 0.0).then_inc(consts, 1)
            pool.memset(mhalf[:, :], -0.5).then_inc(consts, 1)
            pool.memset(upad[:, 0:CONV_W - 1], 0.0).then_inc(consts, 1)
            pool.wait_ge(consts, N_CONST)

            def split_lo(n):
                pool.wait_ge(hi_split, n + 1)
                if n >= N_RING:
                    pool.wait_ge(z_full, chunk_done(n - N_RING))
                pool.tensor_tensor(w_lo[:, n % N_RING, :], stage_of(plan.split[n]),
                                   w_hi[:, n % N_RING, :].bitcast(F32), ALU.subtract).then_inc(lo_split, 1)

            def add_square(tag, m):
                n = (tag + 1) * KT + m
                pool.wait_ge(squared, n + 1)
                if m == 0:
                    pool.tensor_copy(sq_acc, sq_tmp[:, :]).then_inc(sq_added, 1)
                else:
                    pool.wait_ge(sq_added, n)
                    pool.tensor_tensor(sq_acc, sq_acc, sq_tmp[:, :], ALU.add).then_inc(sq_added, 1)

            def root(tag):
                pool.wait_ge(a_dve, plan.freed(plan.aux, aux_no[("ss", tag)])[1])
                pool.tensor_tensor(rt[:, :], ms[:, :], mhalf[:, :], ALU.pow).then_inc(root_ok, 1)

            split_lo(0)
            split_lo(1)
            split = N_RING
            for m in range(KT):
                add_square(-1, m)
            root(-1)
            for st in sched:
                kind = st[0]
                if kind == "OUT":
                    add_square(st[1], st[2])
                elif kind == "NORM":
                    root(st[1])
                elif kind == "GATES":
                    _, l, t = st
                    n = CT * l + t
                    pool.wait_ge(a_ok, n + 1)
                    if n >= 1:
                        pool.wait_ge(m_ok, n)
                    pool.tensor_tensor(SQ, A[t % 2], A[t % 2], ALU.mult).then_inc(sq_ok, 1)
                elif kind == "LRU":
                    _, l, half = st
                    for t in (2 * half, 2 * half + 1):
                        n = CT * l + t
                        pool.wait_ge(ylru_hi, n + 1)
                        pool.tensor_tensor(y_lo[:, t, :], UC[t % 2], y_hi[:, t, :].bitcast(F32),
                                           ALU.subtract).then_inc(ylru_lo, 1)
                elif kind == "ROPE":
                    n = rope_no[st[1:]]
                    pool.wait_ge(swapped, 64 * (n + 1))
                    pool.wait_ge(tab_in, 32)
                    pool.tensor_tensor(swp[:, :], swp[:, :], sinT[:, :], ALU.mult).then_inc(swap_mul, 1)
                for _ in range(plan.steps_ahead(st)):
                    if split < len(plan.split):
                        split_lo(split)
                        split += 1

        @block.scalar
        def _(act):
            def split_hi(n):
                key = plan.split[n]
                act.wait_ge(staged[load_no[key] % N_STAGE], plan.staged_at[key])
                if n >= N_RING:
                    act.wait_ge(z_full, chunk_done(n - N_RING))
                act.activation(w_hi[:, n % N_RING, :], stage_of(key), ACT.Copy).then_inc(hi_split, 1)

            def norm_tile(tag, m):
                n = (tag + 1) * KT + m
                if tag + 1 < DEPTH:
                    col = PG + n
                    act.activation(h_hi[:, m, :], xT[:, m, :], ACT.Copy, scale=par[:, col:col + 1]).then_inc(h_hi_ok, 1)
                if n >= 1:
                    act.wait_ge(sq_added, n)
                act.activation(sq_tmp[:, :], xT[:, m, :], ACT.Square).then_inc(squared, 1)

            def rstd_in(tag):
                act.wait_ge(a_full, aux_no[("rb", tag)] + 1)
                act.activation(rstd[:, :], a_ps[:, :], ACT.Copy).then_inc(a_act, 1)

            def silu_tanh(l, name, n):
                act.wait_ge(z_dve, plan.freed(plan.z, z_no[("Z", l, name)])[1])
                if name == "gl0":
                    act.wait_ge(sq_added, KT * (l + 1))
                if n >= 1:
                    act.wait_ge(silu_ok, n)
                if name == "gn0":
                    act.wait_ge(rot_ok, 6 * (l + 1))
                act.activation(swp[:, :], e_slot((l, name)), ACT.Tanh, scale=0.5).then_inc(gate_tanh, 1)

            split_hi(0)
            split_hi(1)
            split = N_RING
            act.wait_ge(a_dve, 2)
            act.wait_ge(lam_ok, 1)
            act.activation(soft[:, 2, :], soft[:, 1, :], ACT.Exp, scale=-1.0).then_inc(exp_lam, 1)
            for m in range(KT):
                act.wait_ge(z_full, z_no[("X", m)] + 1)
                act.activation(xT[:, m, :], z_bank(("X", m))[:, :], ACT.Copy).then_inc(z_act, 1)
                act.wait_ge(z_act, m + 1)
                norm_tile(-1, m)
            rstd_in(-1)

            for st in sched:
                kind = st[0]
                if kind in ("Z", "OUT") and split < len(plan.split):
                    split_hi(split)
                    split += 1
                if kind == "Z" and stem(st[2]) == "gl":
                    _, l, name = st
                    silu_tanh(l, name, 8 * l + int(name[-1]))
                elif kind == "GATES":
                    _, l, t = st
                    n = CT * l + t
                    if n == 0:
                        act.wait_ge(lru_par, 1)
                    else:
                        act.wait_ge(m_ok, n)
                    act.wait_ge(z_full, z_no[(*st, "a")] + 1)
                    act.activation(THR, z_bank((*st, "a"))[:, :], ACT.Tanh, bias=hba[:, n:n + 1], scale=0.5).then_inc(z_act, 1)
                    act.wait_ge(z_full, z_no[(*st, "i")] + 1)
                    act.activation(THI, z_bank((*st, "i"))[:, :], ACT.Tanh, bias=hbi[:, n:n + 1], scale=0.5).then_inc(z_act, 1)
                    act.wait_ge(z_act, plan.freed(plan.z, z_no[(*st, "i")])[1])
                    act.activation(A[t % 2], THR, ACT.Exp, bias=nsp[:, n:n + 1], scale=nsp[:, n:n + 1]).then_inc(a_ok, 1)
                    act.activation(TH, THR, ACT.Tanh, bias=psp[:, n:n + 1], scale=psp[:, n:n + 1]).then_inc(th_ok, 1)
                elif kind == "LRU":
                    _, l, half = st
                    act.wait_ge(m_ok, CT * l + 2 * half + 2)
                    for t in (2 * half, 2 * half + 1):
                        act.activation(M[t % 2], M[t % 2], ACT.Sqrt, scale=0.25).then_inc(root_m, 1)
                    for t in (2 * half, 2 * half + 1):
                        act.wait_ge(ylru_ok, CT * l + t + 1)
                        if l >= 1 and t == 0:
                            act.wait_ge(z_full, z_no[("OUT", l - 1, KT - 1)] + 1)
                        act.activation(y_hi[:, t, :], UC[t % 2], ACT.Copy).then_inc(ylru_hi, 1)
                elif kind == "CMP":
                    c = 2 * st[1] + st[2]
                    act.wait_ge(hid_in, c + 1)
                    act.activation(hid[:, :, :], hb[:, :, 0:NCOL - 1], ACT.Tanh, scale=0.5).then_inc(hid_tanh, 1)
                elif kind == "ROPE":
                    n = rope_no[st[1:]]
                    act.wait_ge(rot_ok, n + 1)
                    if n >= 1:
                        act.wait_ge(stacked, plan.stacked_at[n - 1])
                    act.activation(r_hi[:, :], e_slot(st[1:]), ACT.Copy).then_inc(rope_hi, 1)
                elif kind == "TURN":
                    _, l, name = st
                    act.wait_ge(a_full, aux_no[st] + 1)
                    if l >= 1:
                        act.wait_ge(pv_done, turns_before(l))
                    if name == "gate":
                        act.activation(gates[:, :, :], a_ps[:, 0:TT * N_GATE].rearrange("p (t n) -> p t n", t=TT),
                                       ACT.Tanh, scale=0.5).then_inc(a_act, 1)
                    else:
                        act.activation(v_sb[:, 0 if name == "vs" else 1, :, :],
                                       a_ps[:, :].rearrange("p (t n) -> p t n", t=TT), ACT.Copy).then_inc(a_act, 1)
                elif kind == "CSOFT":
                    act.wait_ge(cs_sub, st[1] + 1)
                    act.activation(sc[:, :, :, :], sc[:, :, :, :], ACT.Exp, scale=-1.0).then_inc(cs_exp, 1)
                elif kind == "UNIT":
                    _, l, i, b, fill = st
                    u, W = unit_no[(l, i, b)], P * (i + 1)
                    for h in range(8):
                        n = 8 * u + h
                        act.wait_ge(min_ok, n + 1)
                        if h == 0:
                            if u == unit_of_layer(l):
                                act.wait_ge(ylru_lo, CT * (l + 1))
                            if u >= 1:
                                act.wait_ge(t_full, first_turn[(l, i, b)])
                            if u >= 2:
                                act.wait_ge(p_ok, 8 * (u - 1))
                        act.activation(probs[:, h, 0:W], s_ps[n % 2][:, 0:W], ACT.Exp, scale=-1.0,
                                       bias=mn[:, u % 2, h:h + 1], accum_out=rs[:, u % 2, h:h + 1]).then_inc(exp_ok, 1)
                        if fill and h in (3, 7) and split < len(plan.split):
                            split_hi(split)
                            split += 1
                        if fill and h in (5, 7):
                            name = fill[h == 7]
                            silu_tanh(l, name, 8 * l + CT + int(name[-1]))
                    for k in range(plan.turns_of((l, i, b))):
                        n, rows = first_turn[(l, i, b)] + k, P if k <= i else NC
                        act.wait_ge(t_full, n + 1)
                        if n >= 2:
                            act.wait_ge(pv_done, n - 1)
                        act.activation(probsT[0:rows, 2 * (n % 2), :], t_ps[0][0:rows, :], ACT.Copy).then_inc(pt_act, 1)
                    if b == 1:
                        n = TT * l + TT - 1 - i
                        act.wait_ge(ynsa_ok, n + 1)
                        act.activation(y_hi[:, CT:KT, i * P:(i + 1) * P],
                                       e_slot((l, f"y{i}")).rearrange("p (r q) -> p r q", r=GROUP),
                                       ACT.Copy).then_inc(ynsa_hi, 1)
                elif kind == "OUT":
                    _, l, m = st
                    act.wait_ge(x_new, KT * l + m + 1)
                    norm_tile(l, m)
                elif kind == "NORM":
                    rstd_in(st[1])
                elif kind == "FINAL":
                    for m in range(KT):
                        act.wait_ge(z_full, z_no[("F", m)] + 1)
                        act.activation(x_tok[:, :, m * P:(m + 1) * P],
                                       z_bank(("F", m))[:, :].rearrange("p (t n) -> p t n", t=TT),
                                       ACT.Copy).then_inc(tok_ok, 1)

        @block.vector
        def _(dve):
            links = [0]

            def link(ins):
                links[0] += 1
                ins.then_inc(dve_link, 1)
                dve.wait_ge(dve_link, links[0])

            def h_low(tag, m):
                n = (tag + 1) * KT + m
                dve.wait_ge(h_hi_ok, n + 1)
                dve.scalar_tensor_tensor(out=h_lo[:, m, :], in0=xT[:, m, :], scalar=par[:, PG + n:PG + n + 1],
                                         in1=h_hi[:, m, :].bitcast(F32), op0=ALU.mult, op1=ALU.subtract).then_inc(h_lo_ok, 1)

            def mean_square(tag):
                dve.wait_ge(a_full, aux_no[("ss", tag)] + 1)
                dve.tensor_scalar(ms[:, :], a_ps[:, 0:TT], 1.0 / D_MODEL, EPS, ALU.mult, ALU.add).then_inc(a_dve, 1)

            def diagonal(tag):
                dve.wait_ge(root_ok, tag + 2)
                for t in range(TT):
                    ins = dve.tensor_scalar(diag[:, t * P:(t + 1) * P], ident[:, :], rt[:, t:t + 1], None, ALU.mult)
                ins.then_inc(diag_ok, 1)

            def wait_e(key):
                n = e_no[key]
                if n < 2:
                    return
                l, name = plan.e[n - 2]
                if (l, name) in rope_no:
                    dve.wait_ge(rope_lo, rope_no[(l, name)] + 1)
                elif name in ("kc", "vc"):
                    dve.wait_ge(flat_ok, 2 * l + (name == "vc") + 1)
                elif name in ("vs", "vw", "gate"):
                    dve.wait_ge(a_full, aux_no[("TURN", l, name)] + 1)
                elif stem(name) in ("gl", "gn"):
                    dve.wait_ge(silu_ok, 8 * l + (CT if stem(name) == "gn" else 0) + int(name[-1]) + 1)
                elif stem(name) == "y":
                    dve.wait_ge(ynsa_lo, TT * l + TT - int(name[-1]))

            def silu(l, name, n):
                dve.wait_ge(gate_tanh, n + 1)
                dve.scalar_tensor_tensor(out=silu_g[:, int(name[-1]), :], in0=swp[:, :], scalar=1.0,
                                         in1=e_slot((l, name)), op0=ALU.add, op1=ALU.mult).then_inc(silu_ok, 1)

            def projected(st):
                _, l, name = st
                dve.wait_ge(z_full, z_no[st] + 1)
                if stem(name) == "u":
                    dst = upad[:, CONV_W - 1:]
                    before = CT * l + int(name[-1])
                    if before >= 1:
                        dve.wait_ge(conv_ok, before)
                else:
                    wait_e((l, name))
                    dst = e_slot((l, name))
                if name == "gl0":
                    dve.wait_ge(a_act, plan.freed(plan.aux, aux_no[("rb", l - 1)])[1])
                if stem(name) == "q":
                    dve.scalar_tensor_tensor(out=dst, in0=z_bank(st)[:, :], scalar=-(HD ** -0.5), in1=rstd[:, :],
                                             op0=ALU.mult, op1=ALU.mult).then_inc(z_dve, 1)
                else:
                    dve.tensor_tensor(dst, z_bank(st)[:, :], rstd[:, :], ALU.mult).then_inc(z_dve, 1)
                dve.wait_ge(z_dve, plan.freed(plan.z, z_no[st])[1])

            dve.wait_ge(a_full, aux_no["params"] + 1)
            dve.tensor_copy(par[:, :], a_ps[:, 0:NPAR]).then_inc(a_dve, 1)
            dve.wait_ge(a_full, aux_no["pos"] + 1)
            dve.tensor_copy(posT[:, :, :, :], a_ps[:, 0:2 * DEPTH * NPAIR]
                            .rearrange("p (v l j) -> p v l j", v=2, l=DEPTH)).then_inc(a_dve, 1)
            dve.wait_ge(a_dve, 2)
            dve.tensor_scalar(hba[:, :], par[:, PBA:PBA + 8], 0.5, None, ALU.mult)
            dve.tensor_scalar(hbi[:, :], par[:, PBI:PBI + 8], 0.5, None, ALU.mult)
            lam, LG, RC, S2 = par[:, PLAM:PLAM + 8], soft[:, 0, :], soft[:, 3, :], soft[:, 4, :]
            link(dve.tensor_scalar(LG, lam, -1.0, None, ALU.mult))
            dve.tensor_tensor(soft[:, 1, :], lam, LG, ALU.max).then_inc(lam_ok, 1)
            dve.wait_ge(exp_lam, 1)
            link(dve.tensor_scalar(RC, soft[:, 2, :], 2.0, None, ALU.add))
            link(dve.reciprocal(RC, RC))
            link(dve.tensor_tensor(RC, RC, soft[:, 2, :], ALU.mult))
            link(dve.tensor_tensor(S2, RC, RC, ALU.mult))
            link(dve.tensor_scalar(soft[:, 2, :], S2, 1.0 / 19, None, ALU.mult))
            for n in (17, 15, 13, 11, 9, 7, 5, 3):
                link(dve.scalar_tensor_tensor(out=soft[:, 2, :], in0=soft[:, 2, :], scalar=1.0 / n, in1=S2,
                                              op0=ALU.add, op1=ALU.mult))
            link(dve.scalar_tensor_tensor(out=RC, in0=soft[:, 2, :], scalar=1.0, in1=RC, op0=ALU.add, op1=ALU.mult))
            link(dve.tensor_scalar(LG, LG, 0.0, None, ALU.max))
            link(dve.scalar_tensor_tensor(out=LG, in0=RC, scalar=2.0, in1=LG, op0=ALU.mult, op1=ALU.add))
            dve.tensor_scalar(nsp[:, :], LG, -4.0, None, ALU.mult)
            link(dve.tensor_scalar(psp[:, :], LG, 4.0, None, ALU.mult))
            dve.tensor_copy(soft[:, 1, :], psp[:, :]).then_inc(lru_par, 1)
            for m in range(KT):
                h_low(-1, m)
            mean_square(-1)
            diagonal(-1)

            for st in sched:
                kind = st[0]
                if kind == "Z":
                    _, l, name = st
                    projected(st)
                    if stem(name) == "gl":
                        n = 8 * l + int(name[-1])
                        silu(l, name, n)
                    elif stem(name) == "u":
                        t = int(name[-1])
                        n = CT * l + t
                        uc = UC[t % 2]

                        def tap(j):
                            c = PCW + (CONV_W * l + j) * CT + t
                            return upad[:, j:j + SEQ], par[:, c:c + 1]
                        if t >= 2:
                            dve.wait_ge(ylru_lo, n - 1)
                        src, w = tap(0)
                        link(dve.tensor_scalar(uc, src, w, par[:, PCB + n:PCB + n + 1], ALU.mult, ALU.add))
                        for j in range(1, CONV_W):
                            src, w = tap(j)
                            ins = dve.scalar_tensor_tensor(out=uc, in0=src, scalar=w, in1=uc, op0=ALU.mult, op1=ALU.add)
                            if j < CONV_W - 1:
                                link(ins)
                        ins.then_inc(conv_ok, 1)
                elif kind == "GATES":
                    _, l, t = st
                    n = CT * l + t
                    dve.wait_ge(th_ok, n + 1)
                    dve.scalar_tensor_tensor(out=IU[t % 2], in0=THI, scalar=1.0, in1=UC[t % 2], op0=ALU.add, op1=ALU.mult)
                    dve.wait_ge(sq_ok, n + 1)
                    dve.scalar_tensor_tensor(out=M[t % 2], in0=SQ, scalar=1.0, in1=TH, op0=ALU.add, op1=ALU.mult).then_inc(m_ok, 1)
                elif kind == "LRU":
                    _, l, half = st
                    for t in (2 * half, 2 * half + 1):
                        n = CT * l + t
                        dve.wait_ge(root_m, n + 1)
                        link(dve.tensor_tensor(IU[t % 2], IU[t % 2], M[t % 2], ALU.mult))
                        link(dve.tensor_tensor_scan(UC[t % 2], A[t % 2], IU[t % 2], 0.0, ALU.mult, ALU.add))
                        dve.scalar_tensor_tensor(out=UC[t % 2], in0=UC[t % 2], scalar=0.5, in1=silu_g[:, t, :],
                                                 op0=ALU.mult, op1=ALU.mult).then_inc(ylru_ok, 1)
                elif kind == "CMP":
                    _, l, kv = st
                    c = 2 * l + kv
                    src = e_slot((l, "kc" if kv == 0 else "vc"))
                    if c >= 1:
                        dve.wait_ge(a_full, aux_no[("CMP", (c - 1) // 2, (c - 1) % 2, 1)] + 1)
                    if kv == 0 and l >= 1:
                        dve.wait_ge(t_full, turns_before(l))
                    for g in range(N_KV):
                        tokens = src[g * HD:(g + 1) * HD, :].rearrange("p (c j h) -> p h j c", j=NPAIR // 2, h=2)
                        for h in range(2):
                            for a in range(2):
                                dve.tensor_copy(flat[h * HD:(h + 1) * HD, a * 8:a * 8 + 8, g * NC:(g + 1) * NC],
                                                tokens[:, h, :, a:a + NC])
                    dve.tensor_copy(flat[:, :, NCOL - 1:NCOL], posT[:, kv, l, :].rearrange("p (j a) -> p j a", a=1)).then_inc(flat_ok, 1)
                    dve.wait_ge(a_full, aux_no[(*st, 1)] + 1)
                    dve.tensor_copy(hb[:, :, :], a_ps[:, 0:HT * (NCOL + 1)].rearrange("p (m c) -> p m c", m=HT)[:, :, 0:NCOL]).then_inc(a_dve, 1)
                    dve.wait_ge(a_dve, plan.freed(plan.aux, aux_no[(*st, 1)])[1])
                    for m in range(HT):
                        ins = dve.tensor_scalar(hb[:, m, 0:NCOL - 1], hb[:, m, 0:NCOL - 1], hb[:, m, NCOL - 1:NCOL], None, ALU.add)
                    ins.then_inc(hid_in, 1)
                    dve.wait_ge(hid_tanh, c + 1)
                    dve.scalar_tensor_tensor(out=hid[:, :, :], in0=hid[:, :, :], scalar=1.0, in1=hb[:, :, 0:NCOL - 1],
                                             op0=ALU.add, op1=ALU.mult).then_inc(hid_ok, 1)
                    dve.wait_ge(a_full, aux_no[(*st, 2)] + 1)
                    if kv == 0:
                        dve.tensor_scalar(kc_bd[0:HD, 0:NC], a_ps[0:HD, 0:NC], 0.5, None, ALU.mult)
                        dve.tensor_scalar(kc_bd[HD:P, NC:2 * NC], a_ps[HD:P, NC:2 * NC], 0.5, None, ALU.mult).then_inc(a_dve, 1)
                    else:
                        dve.tensor_scalar(vc_sb[:, :, :], a_ps[0:NC, 0:P].rearrange("p (g d) -> p g d", g=N_KV), 0.5, None,
                                          ALU.mult).then_inc(a_dve, 1)
                elif kind == "ROPE":
                    _, l, name = st
                    n, e = rope_no[(l, name)], e_slot((l, name))
                    if stem(name) == "q":
                        r = int(name[-1])
                        dve.wait_ge(a_full, aux_no[st] + 1)
                        dve.tensor_tensor(sc[:, :, 2 * r:2 * r + 2, :],
                                          a_ps[:, 0:TT * N_KV * NC].rearrange("p (i g c) -> p i g c", i=TT, g=N_KV),
                                          mask_c[:, :, :].rearrange("p i (a c) -> p i a c", a=1).to_broadcast([P, TT, N_KV, NC]),
                                          ALU.add).then_inc(a_dve, 1)
                    dve.wait_ge(swapped, 64 * (n + 1))
                    link(dve.tensor_tensor(e, e, cosT[:, :], ALU.mult))
                    dve.wait_ge(swap_mul, n + 1)
                    dve.tensor_tensor(e, e, swp[:, :], ALU.add).then_inc(rot_ok, 1)
                    dve.wait_ge(rope_hi, n + 1)
                    dve.tensor_tensor(r_lo[:, :], e, r_hi[:, :].bitcast(F32), ALU.subtract).then_inc(rope_lo, 1)
                elif kind == "TURN" and st[2] == "gate":
                    dve.wait_ge(a_act, plan.freed(plan.aux, aux_no[st])[1])
                    link(dve.tensor_scalar(gates[:, :, :], gates[:, :, :], 1.0, 0.5, ALU.add, ALU.mult))
                elif kind == "CSOFT":
                    l = st[1]
                    dve.wait_ge(a_dve, plan.freed(plan.aux, aux_no[("ROPE", l, "q3")])[1])
                    link(dve.tensor_reduce(mnc[:, :, :], sc[:, :, :, :], AX.X, ALU.min))
                    sc3 = sc[:, :, :, :].rearrange("p i h c -> p (i h) c")

                    def spread(v):
                        return v[:, :, :].rearrange("p i (h a) -> p (i h) a", a=1).to_broadcast([P, TT * 8, NC])
                    dve.tensor_tensor(sc3, sc3, spread(mnc), ALU.subtract).then_inc(cs_sub, 1)
                    dve.wait_ge(cs_exp, l + 1)
                    link(dve.tensor_reduce(rsc[:, :, :], sc[:, :, :, :], AX.X, ALU.add))
                    link(dve.reciprocal(rsc[:, :, :], rsc[:, :, :]))
                    gate0 = gates[:, :, :].rearrange("p i (g r b) -> p i b r g", g=N_KV, b=3)[:, :, 0, :, :]
                    r4 = rsc[:, :, :].rearrange("p i (r g) -> p i r g", g=N_KV)
                    link(dve.tensor_tensor(r4, r4, gate0, ALU.mult))
                    link(dve.tensor_tensor(rsc[:, :, :], rsc[:, :, :],
                                           row_ok[:, :].rearrange("p (i a) -> p i a", a=1).to_broadcast([P, TT, 8]), ALU.mult))
                    dve.tensor_tensor(sc3, sc3, spread(rsc), ALU.mult).then_inc(cs_ok, 1)
                elif kind == "UNIT":
                    _, l, i, b, fill = st
                    u, W = unit_no[(l, i, b)], P * (i + 1)

                    def row_min(h):
                        n = 8 * u + h
                        dve.wait_ge(s_full, n + 1)
                        dve.tensor_reduce(mn[:, u % 2, h:h + 1], s_ps[n % 2][:, 0:W], AX.X, ALU.min).then_inc(min_ok, 1)

                    def scaled(g):
                        hs = slice(GROUP * g, GROUP * (g + 1))
                        dve.wait_ge(exp_ok, 8 * u + GROUP * (g + 1))
                        link(dve.reciprocal(coef[:, u % 2, hs], rs[:, u % 2, hs]))
                        gate = gates[:, i, :].rearrange("p (h b) -> p b h", b=3)[:, 1 + b, hs]
                        link(dve.tensor_tensor(coef[:, u % 2, hs], coef[:, u % 2, hs], gate, ALU.mult))
                        for h in range(GROUP * g, GROUP * (g + 1)):
                            dve.tensor_scalar(probs[:, h, 0:W], probs[:, h, 0:W], coef[:, u % 2, h:h + 1], None,
                                              ALU.mult).then_inc(p_ok, 1)

                    def gate_in_e(name):
                        projected(("Z", l, name))

                    for h in range(6):
                        row_min(h)
                    scaled(0)
                    if fill:
                        gate_in_e(fill[0])
                    row_min(6)
                    row_min(7)
                    if fill:
                        silu(l, fill[0], 8 * l + CT + int(fill[0][-1]))
                    scaled(1)
                    if fill:
                        gate_in_e(fill[1])
                        silu(l, fill[1], 8 * l + CT + int(fill[1][-1]))
                    for k in range(plan.turns_of((l, i, b))):
                        n, rows = first_turn[(l, i, b)] + k, P if k <= i else NC
                        dve.wait_ge(t_full, n + 1)
                        if n >= 2:
                            dve.wait_ge(pv_done, n - 1)
                        dve.tensor_copy(probsT[0:rows, 2 * (n % 2) + 1, :], t_ps[1][0:rows, :]).then_inc(pt_dve, 1)
                    if b == 1:
                        n = TT * l + TT - 1 - i
                        key = (l, f"y{i}")
                        e = e_slot(key).rearrange("p (r q) -> p r q", r=GROUP)
                        dve.wait_ge(pv_done, first_turn[(l, i, b)] + plan.turns_of((l, i, b)))
                        wait_e(key)
                        dve.scalar_tensor_tensor(out=e, in0=o_ps[:, :].rearrange("p (r q) -> p r q", r=GROUP), scalar=0.5,
                                                 in1=silu_g[:, :, i * P:(i + 1) * P], op0=ALU.mult, op1=ALU.mult).then_inc(ynsa_ok, 1)
                        dve.wait_ge(ynsa_hi, n + 1)
                        dve.tensor_tensor(y_lo[:, CT:KT, i * P:(i + 1) * P], e,
                                          y_hi[:, CT:KT, i * P:(i + 1) * P].bitcast(F32), ALU.subtract).then_inc(ynsa_lo, 1)
                elif kind == "OUT":
                    _, l, m = st
                    dve.wait_ge(z_full, z_no[st] + 1)
                    dve.tensor_tensor(xT[:, m, :], xT[:, m, :], z_bank(st)[:, :], ALU.add).then_inc(x_new, 1)
                    if l + 1 < DEPTH:
                        h_low(l, m)
                elif kind == "NORM":
                    mean_square(st[1])
                    diagonal(st[1])
                elif kind == "FINAL":
                    dve.wait_ge(a_act, plan.freed(plan.aux, aux_no[("rb", DEPTH - 1)])[1])
                    for m in range(KT):
                        dve.scalar_tensor_tensor(out=xT[:, m, :], in0=xT[:, m, :], scalar=par[:, PFG + m:PFG + m + 1],
                                                 in1=rstd[:, :], op0=ALU.mult, op1=ALU.mult).then_inc(fin_ok, 1)

        @block.tensor
        def _(pe):
            def z_product(key, first, last):
                n = split_no[key]
                slot, bank = n % N_RING, z_bank(key)
                l, is_out = key[1], key[0] == "OUT"
                x_hi, x_lo = (y_hi, y_lo) if is_out else (h_hi, h_lo)
                if first == 0:
                    pe.wait_ge(hi_split, n + 1)
                    pe.wait_ge(lo_split, n + 1)
                    wait_z(pe, key)
                for at in range(first, last):
                    k, part = divmod(at, 3)
                    if part == 0 and not is_out and key[2] == "gl0":
                        pe.wait_ge(h_lo_ok, KT * l + k + 1)
                    w = (w_hi, w_hi, w_lo)[part]
                    act_in = (x_hi, x_lo, x_hi)[part]
                    ins = pe.matmul(bank[:, :], w[:, slot, k * P:(k + 1) * P], act_in[:, k, :],
                                    start=(at == 0), stop=(at == 3 * KT - 1))
                if last == 3 * KT:
                    ins.then_inc(z_full, 1)

            def sum_squares(tag):
                wait_aux(pe, ("ss", tag))
                pe.wait_ge(sq_added, KT * (tag + 2))
                for t in range(TT):
                    ins = pe.matmul(a_ps[:, t:t + 1], sq_acc[:, t * P:(t + 1) * P], ones[:, 0:1], start=True, stop=True)
                ins.then_inc(a_full, 1)

            def spread_rstd(tag):
                wait_aux(pe, ("rb", tag))
                pe.wait_ge(diag_ok, tag + 2)
                pe.matmul(a_ps[:, :], ones[:, :], diag, start=True, stop=True).then_inc(a_full, 1)

            def scores(u, h):
                l, i, b = plan.units[u]
                n, W, g = 8 * u + h, P * (i + 1), h // GROUP
                if n >= 2:
                    pe.wait_ge(exp_ok, n - 1)
                q = q_st[:, h, i * P:(i + 1) * P]
                bank = s_ps[n % 2]
                pe.matmul(bank[:, 0:W], q, k_st[:, b, g, 0, 0:W], start=True, stop=False)
                pe.matmul(bank[:, W - P:W], ident_b[:, :], causal_b[:, :], start=False, stop=False)
                pe.matmul(bank[:, 0:W], q, k_st[:, b, g, 1, 0:W], start=False, stop=True).then_inc(s_full, 1)

            def turn(key, k):
                l, i, b = key
                u, n = unit_no[key], first_turn[key] + k
                if n >= 1:
                    pe.wait_ge(pt_act, n)
                    pe.wait_ge(pt_dve, n)
                if k > i:
                    pe.wait_ge(cs_ok, l + 1)
                for g in range(N_KV):
                    if k == 0:
                        pe.wait_ge(p_ok, 8 * u + GROUP * (g + 1))
                    for r in range(GROUP):
                        if k <= i:
                            ins = pe.transpose(t_ps[g][:, r * P:(r + 1) * P], probs[:, GROUP * g + r, k * P:(k + 1) * P], ident[:, :])
                        else:
                            ins = pe.transpose(t_ps[g][0:NC, r * P:(r + 1) * P], sc[:, i, 2 * r + g, :], ident[:, :])
                ins.then_inc(t_full, 1)

            def weigh(key, k):
                l, i, b = key
                n = first_turn[key] + k
                pe.wait_ge(pt_act, n + 1)
                pe.wait_ge(pt_dve, n + 1)
                done = TT * l + TT - 1 - i
                if b == 0 and k == 0 and done >= 1:
                    pe.wait_ge(ynsa_ok, done)
                for g in range(N_KV):
                    if k <= i:
                        v, rows = v_sb[:, b, k, g * HD:(g + 1) * HD], P
                    else:
                        v, rows = vc_sb[:, g, :], NC
                    ins = pe.matmul(o_ps[g * HD:(g + 1) * HD, :], v, probsT[0:rows, 2 * (n % 2) + g, :],
                                    start=(b == 0 and k == 0), stop=(k > i))
                ins.then_inc(pv_done, 1)

            pe.wait_ge(consts, N_CONST)
            pe.wait_ge(par_in, 16 * 9)
            pe.transpose(a_ps[:, 0:NPAR], par_row[0:NPAR, :], ident[0:NPAR, 0:NPAR]).then_inc(a_full, 1)
            wait_aux(pe, "pos")
            n_pos = 2 * DEPTH * NPAIR
            pe.transpose(a_ps[:, 0:n_pos], pos_row[0:n_pos, :], ident[0:n_pos, 0:n_pos]).then_inc(a_full, 1)
            pe.wait_ge(x_in, 16 * TT)
            for m in range(KT):
                wait_z(pe, ("X", m))
                for t in range(TT):
                    ins = pe.transpose(z_bank(("X", m))[:, t * P:(t + 1) * P], x_tok[:, t, m * P:(m + 1) * P], ident[:, :])
                ins.then_inc(z_full, 1)

            for st in sched:
                kind = st[0]
                if kind in ("Z", "OUT"):
                    if kind == "OUT" and st[2] == 0:
                        pe.wait_ge(ylru_lo, CT * (st[1] + 1))
                        pe.wait_ge(ynsa_lo, TT * (st[1] + 1))
                    z_product(st, 0, 3 * KT)
                    if kind == "Z" and st[2] == "gl0":
                        sum_squares(st[1] - 1)
                    if kind == "Z" and st[2] == "gl1":
                        spread_rstd(st[1] - 1)
                elif kind == "NORM" and st[1] == DEPTH - 1:
                    sum_squares(st[1])
                    spread_rstd(st[1])
                elif kind == "GATES":
                    _, l, t = st
                    pe.wait_ge(conv_ok, CT * l + t + 1)
                    if t == 0:
                        pe.wait_ge(small_in, 96 * (l + 1))
                    for ab, which in enumerate("ai"):
                        wait_z(pe, (*st, which))
                        pe.matmul(z_bank((*st, which))[:, :], bd[:, t, ab, :], UC[t % 2], start=True, stop=True).then_inc(z_full, 1)
                elif kind == "CMP":
                    _, l, kv = st
                    c = 2 * l + kv
                    wait_aux(pe, (*st, 1))
                    pe.wait_ge(flat_ok, c + 1)
                    for part in range(4):
                        key = (*st, part)
                        pe.wait_ge(staged[load_no[key] % N_STAGE], plan.staged_at[key])
                        w1 = stage_of(key).rearrange("p (j n) -> p j n", j=4)
                        for j in range(4):
                            for m in range(HT):
                                ins = pe.matmul(a_ps[:, m * (NCOL + 1):m * (NCOL + 1) + NCOL], w1[:, j, m * P:(m + 1) * P],
                                                flat[:, 4 * part + j, :], start=(part == j == m == 0),
                                                stop=(part == 3 and j == 3), skip_group_check=True)
                        ins.then_inc(a_full if part == 3 else cmp_used, 1)
                    wait_aux(pe, (*st, 2))
                    pe.wait_ge(small_in, 96 * (l + 1))
                    pe.wait_ge(hid_ok, c + 1)
                    for g in range(N_KV):
                        for m in range(HT):
                            h = hid[:, m, g * NC:(g + 1) * NC]
                            if kv == 0:
                                o, a, b = a_ps[g * HD:(g + 1) * HD, g * NC:(g + 1) * NC], w2[:, kv, m, :], h
                            else:
                                o, a, b = a_ps[0:NC, g * HD:(g + 1) * HD], h, w2[:, kv, m, :]
                            ins = pe.matmul(o, a, b, start=(m == 0), stop=(m == HT - 1), skip_group_check=True)
                    ins.then_inc(a_full, 1)
                elif kind == "TURN":
                    _, l, name = st
                    who, count = plan.freed(plan.z, z_no[("Z", l, name)])
                    pe.wait_ge(z_free[who], count)
                    wait_aux(pe, st)
                    e = e_slot((l, name))
                    rows = N_GATE if name == "gate" else P
                    for t in range(TT):
                        ins = pe.transpose(a_ps[:, t * rows:(t + 1) * rows], e[0:rows, t * P:(t + 1) * P], ident[0:rows, 0:rows])
                    ins.then_inc(a_full, 1)
                elif kind == "ROPE" and stem(st[2]) == "q":
                    _, l, name = st
                    who, count = plan.freed(plan.z, z_no[("Z", l, name)])
                    pe.wait_ge(z_free[who], count)
                    wait_aux(pe, st)
                    for i in range(TT):
                        ins = pe.matmul(a_ps[:, i * N_KV * NC:(i + 1) * N_KV * NC], e_slot((l, name))[:, i * P:(i + 1) * P],
                                        kc_bd[:, :], start=True, stop=True)
                    ins.then_inc(a_full, 1)
                elif kind == "UNIT":
                    _, l, i, b, fill = st
                    key = (l, i, b)
                    u = unit_no[key]
                    if u == unit_of_layer(l):
                        pe.wait_ge(stacked, plan.stacked_at[6 * l + 5])
                    for h in range(8):
                        scores(u, h)
                        if fill and 1 <= h <= 6:
                            which, part = divmod(h - 1, 3)
                            z_product(("Z", l, fill[which]), part * KT, (part + 1) * KT)
                    turns = plan.turns_of(key)
                    for k in range(turns):
                        turn(key, k)
                        if k >= 1:
                            weigh(key, k - 1)
                    weigh(key, turns - 1)
                elif kind == "FINAL":
                    for m in range(KT):
                        wait_z(pe, ("F", m))
                        pe.wait_ge(fin_ok, m + 1)
                        for t in range(TT):
                            ins = pe.transpose(z_bank(("F", m))[:, t * P:(t + 1) * P], xT[:, m, t * P:(t + 1) * P], ident[:, :])
                        ins.then_inc(z_full, 1)


_INS = ["x", "norm_g", "w_in", "conv_w", "conv_b", "lru_wa", "lru_ba", "lru_wi", "lru_bi", "lru_lambda",
        "cmp_pos_k", "cmp_pos_v", "cmp_k_w1", "cmp_k_w2", "cmp_v_w1", "cmp_v_w2", "w_out", "final_g"]


def rope_tables():
    inv = np.float32(1.0) / np.float32(10000.0) ** (np.arange(0, HD, 2, dtype=np.float32) / np.float32(HD))
    ang = (np.arange(SEQ, dtype=np.float32)[:, None] * inv[None, :].astype(np.float32)).astype(np.float32)
    c, s = np.cos(ang).T.astype(np.float32), np.sin(ang).T.astype(np.float32)
    return np.ascontiguousarray(np.concatenate([c] * 4)), np.ascontiguousarray(np.concatenate([-s, s] * 2))


def kernel(**inputs):
    import concourse.bacc as bacc
    from concourse.bass_utils import run_bass_kernel_spmd

    nc = bacc.Bacc("TRN2", target_bir_lowering=False, num_devices=1)
    arrays, args = {}, []
    named = [(name, np.ascontiguousarray(inputs[name])) for name in _INS]
    for name, a in [*named, *zip(("rope_cos", "rope_sin"), rope_tables())]:
        arrays[f"in_{name}"] = a
        args.append(nc.dram_tensor(f"in_{name}", a.shape, mybir.dt.from_np(a.dtype), kind="ExternalInput").ap())
    args.append(nc.dram_tensor("out", (1, SEQ, D_MODEL), F32, kind="ExternalOutput").ap())
    hybrid_trunk(nc, *args)
    return run_bass_kernel_spmd(nc, [arrays], core_ids=[0]).results[0]["out"]
```

```python
from contextlib import ExitStack

import numpy as np

import concourse.bass as bass
from concourse import mybir

F32, F32R, BF16 = mybir.dt.float32, mybir.dt.float32r, mybir.dt.bfloat16
ALU, ACT, AX = mybir.AluOpType, mybir.ActivationFunctionType, mybir.AxisListType

P = 128
D_MODEL, SEQ, DEPTH = 1024, 512, 2
D_LRU = D_NSA = 512
LRU_BLK, CONV_W = 64, 4
HD, N_KV, GROUP = 64, 2, 4
CMP_LEN, CMP_STRIDE, CMP_HID = 32, 16, 256
EPS, BIG = 1e-6, 1e30
KT = D_MODEL // P
TT = SEQ // P
CT = D_LRU // P
NC = SEQ // CMP_STRIDE - CMP_LEN // CMP_STRIDE + 1
NPAIR = CMP_LEN // 2
NCOL = N_KV * NC + 1
HT = CMP_HID // P
COL_U, COL_GL, COL_Q, COL_GN = 0, 512, 1024, 1536
COL_KC, COL_VC, COL_KS, COL_VS, COL_KW, COL_VW, COL_GATE = 2048, 2176, 2304, 2432, 2560, 2688, 2816
N_GATE = 24
PG, PFG, PCW, PCB, PBA, PBI, PLAM, NPAR = 0, 16, 24, 56, 64, 72, 80, 88
N_STAGE, N_RING, N_PT, N_E = 3, 2, 4, 3
FILL = {0: ("gn1",), 1: ("gn2",), 2: ("gn3",)}


def schedule():
    s = []
    for l in range(DEPTH):
        def z(*names):
            s.extend(("Z", l, name) for name in names)

        def c1(kv, *parts):
            s.extend(("C1", l, kv, part) for part in parts)

        z("gl0", "gl1", "kc")
        s.append(("FLAT", l, 0))
        z("vc")
        c1(0, 0, 1)
        z("u0")
        c1(0, 2, 3)
        s.append(("SILU", l, 0))
        z("u1")
        s.extend([("HID", l, 0), ("FLAT", l, 1), ("GATES", l, 0)])
        z("gl2")
        c1(1, 0, 1)
        s.append(("GATES", l, 1))
        z("gl3")
        c1(1, 2, 3)
        s.append(("SILU", l, 1))
        z("ks")
        s.extend([("HID", l, 1), ("LRU", l, 0)])
        z("u2")
        s.append(("ROPE", l, "ks"))
        z("kw")
        s.extend([("LOW", l, "ks"), ("GATES", l, 2)])
        z("u3")
        s.append(("ROPE", l, "kw"))
        z("q0")
        s.extend([("LOW", l, "kw"), ("GATES", l, 3)])
        z("vs")
        s.append(("LRU", l, 1))
        s.append(("ROPE", l, "q0"))
        z("q1")
        s.extend([("LOW", l, "q0"), ("TURN", l, "vs")])
        z("vw")
        s.append(("ROPE", l, "q1"))
        z("q2")
        s.extend([("LOW", l, "q1"), ("TURN", l, "vw")])
        z("gate")
        s.append(("ROPE", l, "q2"))
        z("q3")
        s.extend([("LOW", l, "q2"), ("TURN", l, "gate")])
        z("gn0")
        s.extend([("ROPE", l, "q3"), ("LOW", l, "q3")])
        n = 0
        for i in reversed(range(TT)):
            for b in range(2):
                for pair in range(2):
                    s.append(("UNIT", l, (i, b, pair), FILL.get(n, ())))
                    n += 1
                    if n == 3:
                        s.append(("CSOFT", l))
        s.append(("UNIT", l, None, ()))
        s += [("OUT", l, m) for m in range(KT)]
        s.append(("NORM", l))
    s.append(("FINAL",))
    return s


def stem(name):
    return name.rstrip("0123")


class Plan:

    def __init__(self, sched):
        self.split = []
        self.z = [(("X", m), "dve") for m in range(KT)]
        self.aux = [("params", "dve"), ("pos", "dve"), (("ss", -1), "dve"), (("rb", -1), "act")]
        self.e = []
        last = None
        for st in sched:
            k = st[0]
            if k in ("Z", "OUT"):
                self.chunk(st)
                if k == "Z" and stem(st[2]) != "u":
                    self.e.append(st[1:])
            elif k == "GATES":
                self.z += [((*st, "a"), "act"), ((*st, "i"), "act")]
            elif k == "C1" and st[3] == 3:
                self.aux.append((("C1", st[1], st[2]), "dve"))
            elif k == "HID":
                self.aux.append((st, "dve"))
            elif k == "TURN":
                self.aux.append((st, "act"))
            elif k == "ROPE" and stem(st[2]) == "q":
                self.aux.append((st, "dve"))
            elif k == "UNIT":
                for name in st[3]:
                    self.chunk(("Z", st[1], name))
                    self.e.append((st[1], name))
                if last and last[1:] == (1, 1):
                    self.e.append((st[1], f"y{last[0]}"))
                last = st[2]
            elif k == "NORM":
                self.aux += [(("ss", st[1]), "dve"), (("rb", st[1]), "act")]
            elif k == "FINAL":
                self.z += [(("F", m), "tok") for m in range(KT)]
        self.loads, n = self.split[:N_RING], N_RING
        for st in sched:
            if st[0] == "C1":
                self.loads.append(st)
            steps = self.steps_ahead(st)
            self.loads += self.split[n:n + steps]
            n += steps
        self.split_no = {key: n for n, key in enumerate(self.split)}
        self.load_no = {key: n for n, key in enumerate(self.loads)}
        self.z_no = {key: n for n, (key, _) in enumerate(self.z)}
        self.aux_no = {key: n for n, (key, _) in enumerate(self.aux)}
        self.e_no = {key: n for n, key in enumerate(self.e)}
        self.rope = [st[1:] for st in sched if st[0] == "ROPE"]
        self.rope_no = {key: n for n, key in enumerate(self.rope)}
        self.units = [(st[1], *st[2]) for st in sched if st[0] == "UNIT" and st[2]]
        self.unit_no = {key: n for n, key in enumerate(self.units)}
        self.turns, self.first_turn = 0, {}
        for key in self.units:
            self.first_turn[key] = self.turns
            self.turns += self.turns_of(key)
        self.silus, self.ropes, n_silu, n_rope = {}, {}, 0, 0
        for st in sched:
            names = st[2:] if st[0] == "Z" else st[3] if st[0] == "UNIT" else ()
            for name in names:
                if stem(name) in ("gl", "gn"):
                    self.silus[(st[1], name)], self.ropes[(st[1], name)] = n_silu, n_rope
                    n_silu += 1
            if st[0] == "ROPE":
                self.silus[st], self.ropes[st] = n_silu, n_rope
                n_rope += 1
        self.staged_at, count = {}, [0] * N_STAGE
        for n, key in enumerate(self.loads):
            count[n % N_STAGE] += 16 * self.pieces(key)
            self.staged_at[key] = count[n % N_STAGE]

    def chunk(self, st):
        self.split.append(st)
        self.z.append((st, "out" if st[0] == "OUT" else "dve"))

    @staticmethod
    def steps_ahead(st):
        return 1 if st[0] in ("Z", "OUT") else len(st[3]) if st[0] == "UNIT" else 0

    @staticmethod
    def turns_of(key):
        _, i, b, _ = key
        return i + 1 + (b == 1)

    @staticmethod
    def unit_order(turns):
        order = [("S", 0), ("S", 1), ("S", 2)]
        for k in range(turns + 1):
            if k < turns:
                order.append(("T", k))
            if k == 0:
                order.append(("S", 3))
            if 1 <= k <= turns:
                order.append(("W", k - 1))
        return order

    @staticmethod
    def pieces(key):
        if key[0] == "OUT":
            return 3
        return 2 if key[0] == "Z" and stem(key[2]) in ("q", "gn", "gate") else 1

    def freed(self, uses, n):
        who = uses[n][1]
        return who, sum(w == who for _, w in uses[:n + 1])


def hybrid_trunk(nc, x, norm_g, w_in, conv_w, conv_b, lru_wa, lru_ba, lru_wi, lru_bi, lru_lambda,
                 cmp_pos_k, cmp_pos_v, cmp_k_w1, cmp_k_w2, cmp_v_w1, cmp_v_w2, w_out, final_g,
                 rope_cos, rope_sin, out):
    sched = schedule()
    plan = Plan(sched)
    split_no, load_no, z_no, aux_no, e_no = plan.split_no, plan.load_no, plan.z_no, plan.aux_no, plan.e_no
    rope_no, unit_no, first_turn = plan.rope_no, plan.unit_no, plan.first_turn

    ctx = ExitStack()
    with ctx:
        def sb(name, shape, dt=F32):
            return ctx.enter_context(nc.sbuf_tensor(name, shape, dt))

        def sem(name):
            return ctx.enter_context(nc.semaphore(name))

        def psum(name, n):
            return [ctx.enter_context(nc.psum_tensor(f"{name}{k}", [P, SEQ], F32)) for k in range(n)]

        xT = sb("xT", [P, KT, SEQ])
        h_hi, h_lo = sb("h_hi", [P, KT, SEQ], F32R), sb("h_lo", [P, KT, SEQ], F32R)
        y_hi, y_lo = sb("y_hi", [P, KT, SEQ], F32R), sb("y_lo", [P, KT, SEQ], F32R)
        stage = sb("stage", [P, N_STAGE, KT * P])
        w_hi, w_lo = sb("w_hi", [P, N_RING, KT * P], F32R), sb("w_lo", [P, N_RING, KT * P], F32R)
        probs = sb("probs", [P, 8, SEQ])
        probsT = sb("probsT", [P, N_PT, SEQ])
        q_st = sb("q_st", [P, 8, SEQ], F32R)
        k_st = sb("k_st", [P, 2, N_KV, 2, SEQ], F32R)
        v_sb = sb("v_sb", [P, 2, TT, P])
        silu_g = sb("silu_g", [P, 4, SEQ])
        cosT, sinT = sb("cosT", [P, SEQ]), sb("sinT", [P, SEQ])
        ident, ones = sb("ident", [P, P]), sb("ones", [P, P])
        ident_b, causal_b = sb("ident_b", [P, P], BF16), sb("causal_b", [P, P], BF16)
        E = sb("E", [P, N_E, SEQ])
        swp = sb("swp", [P, SEQ])
        rstd = sb("rstd", [P, SEQ])
        upad = sb("upad", [P, SEQ + CONV_W - 1])
        cmpb = sb("cmpb", [P, NPAIR * NCOL])
        bd = sb("bd", [P, CT, 2, P])
        w2 = sb("w2", [P, 2, HT, HD])
        par, posT = sb("par", [P, NPAR]), sb("posT", [P, 2, DEPTH, NPAIR])
        hb, hid = sb("hb", [P, HT, NCOL]), sb("hid", [P, HT, NCOL - 1])
        kc_bd, vc_sb = sb("kc_bd", [P, N_KV * NC]), sb("vc_sb", [NC, N_KV, HD])
        mask_c, row_ok = sb("mask_c", [P, TT, NC]), sb("row_ok", [P, TT])
        gates = sb("gates", [P, TT, N_GATE])
        mn, rs, coef = sb("mn", [P, 2, 4]), sb("rs", [P, 2, 4]), sb("coef", [P, 2, 4])
        mnc, rsc = sb("mnc", [P, TT, 8]), sb("rsc", [P, TT, 8])
        soft = sb("soft", [P, 5, 8])
        nsp, psp = sb("nsp", [P, 8]), sb("psp", [P, 8])
        hba, hbi = sb("hba", [P, 8]), sb("hbi", [P, 8])
        ms, mhalf, rt = sb("ms", [P, TT]), sb("mhalf", [P, TT]), sb("rt", [P, TT])

        par_row, pos_row = E[:, 0, 0:P], E[:, 0, P:2 * P]
        flat = cmpb[:, :].rearrange("p (j c) -> p j c", c=NCOL)
        sc = cmpb[:, 0:TT * 8 * NC].rearrange("p (i h c) -> p i h c", i=TT, c=NC)
        x_tok = probs[:, :, :].rearrange("p (t a) n -> p t (a n)", t=TT)
        sq_tmp, sq_acc = swp, upad[:, CONV_W - 1:]
        diag = probs[:, 0, :]
        UC, A = [probs[:, 0, :], probs[:, 1, :]], [probs[:, 2, :], probs[:, 3, :]]
        M, IU = [probs[:, 4, :], probs[:, 5, :]], [probs[:, 6, :], probs[:, 7, :]]
        THR, THI, TH, SQ = (probsT[:, n, :] for n in range(4))

        z_ps, s_ps, t_ps = psum("z_ps", 2), psum("s_ps", 2), psum("t_ps", 2)
        (o_ps,), (a_ps,) = psum("o_ps", 1), psum("a_ps", 1)
        s_ps.append(a_ps)

        x_in, par_in, tab_in, small_in = sem("x_in"), sem("par_in"), sem("tab_in"), sem("small_in")
        staged = [sem(f"staged{k}") for k in range(N_STAGE)]
        stored = sem("stored")
        hi_split, lo_pool, lo_dve, cmp_used = sem("hi_split"), sem("lo_pool"), sem("lo_dve"), sem("cmp_used")
        z_full, z_dve, z_act = sem("z_full"), sem("z_dve"), sem("z_act")
        a_full, a_dve, a_act = sem("a_full"), sem("a_dve"), sem("a_act")
        s_full, t_full = sem("s_full"), sem("t_full")
        dve_link, pool_link = sem("dve_link"), sem("pool_link")
        first_consts = sem("first_consts")
        consts, lam_ok, exp_lam, lru_par = sem("consts"), sem("lam_ok"), sem("exp_lam"), sem("lru_par")
        x_new, h_hi_ok, h_lo_ok = sem("x_new"), sem("h_hi_ok"), sem("h_lo_ok")
        squared, sq_added, root_ok, diag_ok = sem("squared"), sem("sq_added"), sem("root_ok"), sem("diag_ok")
        gate_tanh, silu_ok = sem("gate_tanh"), sem("silu_ok")
        conv_ok, a_ok, th_ok, sq_ok, m_ok, root_m = sem("conv_ok"), sem("a_ok"), sem("th_ok"), sem("sq_ok"), sem("m_ok"), sem("root_m")
        ylru_ok, ylru_hi, ylru_lo = sem("ylru_ok"), sem("ylru_hi"), sem("ylru_lo")
        flat_ok, hid_in, hid_tanh, hid_ok = sem("flat_ok"), sem("hid_in"), sem("hid_tanh"), sem("hid_ok")
        rot_ok, rope_hi, rope_lo = sem("rot_ok"), sem("rope_hi"), sem("rope_lo")
        cs_sub, cs_exp, cs_ok = sem("cs_sub"), sem("cs_exp"), sem("cs_ok")
        min_ok, exp_ok, p_ok, pt_act, pt_dve, pv_done = sem("min_ok"), sem("exp_ok"), sem("p_ok"), sem("pt_act"), sem("pt_dve"), sem("pv_done")
        ynsa_ok, ynsa_hi, ynsa_lo = sem("ynsa_ok"), sem("ynsa_hi"), sem("ynsa_lo")
        fin_ok, tok_ok = sem("fin_ok"), sem("tok_ok")

        z_free, a_free = {"dve": z_dve, "act": z_act, "out": x_new, "tok": tok_ok}, {"dve": a_dve, "act": a_act}
        N_CONST = 8

        def wait_z(eng, key):
            n = z_no[key]
            if n >= 2:
                who, count = plan.freed(plan.z, n - 2)
                eng.wait_ge(z_free[who], count)

        def wait_aux(eng, key):
            n = aux_no[key]
            if n >= 1:
                who, count = plan.freed(plan.aux, n - 1)
                eng.wait_ge(a_free[who], count)

        def z_bank(key):
            return z_ps[z_no[key] % 2]

        def e_slot(key):
            return E[:, e_no[key] % N_E, :]

        def stage_of(key):
            return stage[:, load_no[key] % N_STAGE, :]

        def units_before(l):
            return 4 * TT * l

        def turns_before(l):
            return plan.turns // DEPTH * l

        def wait_low(eng, n):
            is_out = plan.split[n][0] == "OUT"
            count = sum((key[0] == "OUT") == is_out for key in plan.split[:n + 1])
            eng.wait_ge(lo_dve if is_out else lo_pool, count)

        def head(unit, j):
            return GROUP * (j // 2) + 2 * unit[3] + j % 2

        def wait_turned(eng, n):
            eng.wait_ge(pt_dve if n % 2 else pt_act, n // 2 + 1)

        def chunk_done(n):
            return z_no[plan.split[n]] + 1

        block = ctx.enter_context(nc.Block())

        @block.sync
        def _(sync):
            for t in range(0, TT, 2):
                sync.dma_start(x_tok[:, t, :], x[0, t * P:(t + 1) * P, :]).then_inc(x_in, 16)
            for at, src in ((PG, norm_g.rearrange("l (m p) -> (l m) p", p=P)),
                            (PFG, final_g.rearrange("(m p) -> m p", p=P)),
                            (PCW, conv_w.rearrange("l j (t p) -> (l j t) p", p=P)),
                            (PCB, conv_b.rearrange("l (t p) -> (l t) p", p=P)),
                            (PBA, lru_ba.rearrange("l (t p) -> (l t) p", p=P)),
                            (PBI, lru_bi.rearrange("l (t p) -> (l t) p", p=P)),
                            (PLAM, lru_lambda.rearrange("l (t p) -> (l t) p", p=P))):
                sync.dma_start(par_row[at:at + src.shape[0], :], src).then_inc(par_in, 16)
            for kv, pos in enumerate((cmp_pos_k, cmp_pos_v)):
                n = DEPTH * NPAIR
                sync.dma_start(pos_row[kv * n:(kv + 1) * n, :],
                               pos.rearrange("l (j h) d -> (l j) (h d)", h=2)).then_inc(par_in, 16)

            def load(n):
                key = plan.loads[n]
                if n >= N_STAGE:
                    old = plan.loads[n - N_STAGE]
                    if old[0] == "C1":
                        if old[3] == 3:
                            sync.wait_ge(a_full, aux_no[old[:3]] + 1)
                        else:
                            sync.wait_ge(cmp_used, 3 * (2 * old[1] + old[2]) + old[3] + 1)
                    else:
                        sync.wait_ge(hi_split, split_no[old] + 1)
                        wait_low(sync, split_no[old])
                slot, done = stage_of(key), staged[n % N_STAGE]
                if key[0] == "C1":
                    _, l, kv, c = key
                    w = (cmp_k_w1, cmp_v_w1)[kv][l]
                    sync.dma_start(slot.rearrange("p (j n) -> p j n", j=4),
                                   w[c * 4 * P:(c + 1) * 4 * P, :].rearrange("(j p) n -> p j n", p=P)).then_inc(done, 16)
                    return
                dst = slot.rearrange("p (k n) -> p k n", k=KT)
                if key[0] == "OUT":
                    _, l, m = key
                    cols = w_out[l][:, m * P:(m + 1) * P]
                    sync.dma_start(dst[:, 0:CT, :], cols[0:D_LRU, :].rearrange("(k p) n -> p k n", p=P)).then_inc(done, 16)
                    for g in range(N_KV):
                        sync.dma_start(dst[g * HD:(g + 1) * HD, CT:KT, :],
                                       cols[D_LRU + g * GROUP * HD:D_LRU + (g + 1) * GROUP * HD, :]
                                       .rearrange("(r d) n -> d r n", d=HD)).then_inc(done, 16)
                    return
                _, l, name = key
                w = w_in[l].rearrange("(k p) n -> p k n", p=P)
                if stem(name) in ("q", "gn"):
                    at = (COL_Q if stem(name) == "q" else COL_GN) + int(name[-1]) * HD
                    for g in range(N_KV):
                        src = w[:, :, at + g * GROUP * HD:at + g * GROUP * HD + HD]
                        sync.dma_start(dst[:, :, g * HD:(g + 1) * HD], src).then_inc(done, 16)
                elif name == "gate":
                    sync.dma_start(dst[:, :, 0:N_GATE], w[:, :, COL_GATE:COL_GATE + N_GATE]).then_inc(done, 16)
                    sync.dma_start(dst[:, :, N_GATE:P], w[:, :, COL_GATE - P + N_GATE:COL_GATE]).then_inc(done, 16)
                else:
                    at = {"u": COL_U, "gl": COL_GL, "kc": COL_KC, "vc": COL_VC, "ks": COL_KS, "vs": COL_VS,
                          "kw": COL_KW, "vw": COL_VW}[stem(name)]
                    at += int(name[-1]) * P if name[-1].isdigit() else 0
                    sync.dma_start(dst, w[:, :, at:at + P]).then_inc(done, 16)

            def small_weights(l):
                if l == 0:
                    sync.wait_ge(consts, N_CONST)
                else:
                    sync.wait_ge(z_full, z_no[("GATES", l - 1, CT - 1, "i")] + 1)
                    sync.wait_ge(a_dve, plan.freed(plan.aux, aux_no[("HID", l - 1, 1)])[1])
                for ab, w in enumerate((lru_wa, lru_wi)):
                    for h in range(2):
                        sync.dma_start(bd[h * HD:(h + 1) * HD, :, ab, h * HD:(h + 1) * HD],
                                       w[l].rearrange("(t h) i j -> h i t j", h=2)[h]).then_inc(small_in, 16)
                for kv, w in enumerate((cmp_k_w2, cmp_v_w2)):
                    sync.dma_start(w2[:, kv, :, :], w[l].rearrange("(m p) d -> p m d", p=P)).then_inc(small_in, 16)

            for n in range(N_STAGE):
                load(n)
            loaded = N_STAGE
            sync.dma_start(cosT[:, :], rope_cos).then_inc(tab_in, 16)
            sync.dma_start(sinT[:, :], rope_sin).then_inc(tab_in, 16)
            small_weights(0)
            for st in sched:
                kind = st[0]
                for _ in range(1 if kind == "C1" else plan.steps_ahead(st)):
                    if loaded < len(plan.loads):
                        load(loaded)
                        loaded += 1
                if kind == "CSOFT" and st[1] + 1 < DEPTH:
                    small_weights(st[1] + 1)
            for m in range(KT):
                sync.wait_ge(tok_ok, m + 1)
                sync.dma_start(out[0].rearrange("(t p) n -> p t n", p=P)[:, :, m * P:(m + 1) * P],
                               x_tok[:, :, m * P:(m + 1) * P]).then_inc(stored, 16)
            sync.wait_ge(stored, 16 * KT)

        @block.gpsimd
        def _(pool):
            links = [0]

            def link(ins):
                links[0] += 1
                ins.then_inc(pool_link, 1)
                pool.wait_ge(pool_link, links[0])

            link(pool.memset(ident[:, :], 0.0))
            link(pool.affine_select(out=ident[:, :], in_=ident[:, :], compare_op=ALU.not_equal, fill=1.0,
                                    base=0, pattern=[[-1, P]], channel_multiplier=1))
            pool.memset(ones[:, :], 1.0).then_inc(first_consts, 1)
            pool.tensor_copy(ident_b[:, :], ident[:, :]).then_inc(consts, 1)
            pool.memset(bd[:, :, :, :], 0.0).then_inc(consts, 1)
            link(pool.memset(causal_b[:, :], 0.0))
            pool.affine_select(out=causal_b[:, :], in_=causal_b[:, :], compare_op=ALU.is_ge, fill=BIG, base=0,
                               pattern=[[-1, P]], channel_multiplier=1).then_inc(consts, 1)
            link(pool.memset(mask_c[:, :, :], 0.0))
            pool.affine_select(out=mask_c[:, :, :], in_=mask_c[:, :, :], compare_op=ALU.is_ge, fill=BIG,
                               base=-(CMP_LEN - 1), pattern=[[P, TT], [-CMP_STRIDE, NC]],
                               channel_multiplier=1).then_inc(consts, 1)
            link(pool.memset(row_ok[:, :], 1.0))
            pool.affine_select(out=row_ok[:, :], in_=row_ok[:, :], compare_op=ALU.is_ge, fill=0.0,
                               base=-(CMP_LEN - 1), pattern=[[P, TT]], channel_multiplier=1).then_inc(consts, 1)
            pool.memset(kc_bd[:, :], 0.0).then_inc(consts, 1)
            pool.memset(mhalf[:, :], -0.5).then_inc(consts, 1)
            pool.memset(upad[:, 0:CONV_W - 1], 0.0).then_inc(consts, 1)
            pool.wait_ge(consts, N_CONST)

            def split_lo(n):
                pool.wait_ge(hi_split, n + 1)
                if n >= N_RING:
                    pool.wait_ge(z_full, chunk_done(n - N_RING))
                pool.tensor_tensor(w_lo[:, n % N_RING, :], stage_of(plan.split[n]),
                                   w_hi[:, n % N_RING, :].bitcast(F32), ALU.subtract).then_inc(lo_pool, 1)

            def add_square(tag, m):
                n = (tag + 1) * KT + m
                pool.wait_ge(squared, n + 1)
                if m == 0:
                    pool.tensor_copy(sq_acc, sq_tmp[:, :]).then_inc(sq_added, 1)
                else:
                    pool.wait_ge(sq_added, n)
                    pool.tensor_tensor(sq_acc, sq_acc, sq_tmp[:, :], ALU.add).then_inc(sq_added, 1)

            def root(tag):
                pool.wait_ge(a_dve, plan.freed(plan.aux, aux_no[("ss", tag)])[1])
                pool.tensor_tensor(rt[:, :], ms[:, :], mhalf[:, :], ALU.pow).then_inc(root_ok, 1)

            split_lo(0)
            split_lo(1)
            split = N_RING
            for m in range(KT):
                add_square(-1, m)
            root(-1)
            for st in sched:
                kind = st[0]
                if kind == "OUT":
                    add_square(st[1], st[2])
                elif kind == "NORM":
                    root(st[1])
                elif kind == "GATES":
                    _, l, t = st
                    n = CT * l + t
                    pool.wait_ge(a_ok, n + 1)
                    if n >= 1:
                        pool.wait_ge(m_ok, n)
                    pool.tensor_tensor(SQ, A[t % 2], A[t % 2], ALU.mult).then_inc(sq_ok, 1)
                elif kind == "LRU":
                    _, l, half = st
                    for t in (2 * half, 2 * half + 1):
                        n = CT * l + t
                        pool.wait_ge(ylru_hi, n + 1)
                        pool.tensor_tensor(y_lo[:, t, :], UC[t % 2], y_hi[:, t, :].bitcast(F32),
                                           ALU.subtract).then_inc(ylru_lo, 1)
                for _ in range(plan.steps_ahead(st)):
                    if split < len(plan.split):
                        if plan.split[split][0] == "Z":
                            split_lo(split)
                        split += 1

        @block.scalar
        def _(act):
            def split_hi(n):
                key = plan.split[n]
                act.wait_ge(staged[load_no[key] % N_STAGE], plan.staged_at[key])
                if n >= N_RING:
                    act.wait_ge(z_full, chunk_done(n - N_RING))
                act.activation(w_hi[:, n % N_RING, :], stage_of(key), ACT.Copy).then_inc(hi_split, 1)

            def norm_tile(tag, m):
                n = (tag + 1) * KT + m
                if tag + 1 < DEPTH:
                    col = PG + n
                    act.activation(h_hi[:, m, :], xT[:, m, :], ACT.Copy, scale=par[:, col:col + 1]).then_inc(h_hi_ok, 1)
                if n >= 1:
                    act.wait_ge(sq_added, n)
                act.activation(sq_tmp[:, :], xT[:, m, :], ACT.Square).then_inc(squared, 1)

            def rstd_in(tag):
                act.wait_ge(a_full, aux_no[("rb", tag)] + 1)
                act.activation(rstd[:, :], a_ps[:, :], ACT.Copy).then_inc(a_act, 1)

            def silu_tanh(l, name, n):
                act.wait_ge(z_dve, plan.freed(plan.z, z_no[("Z", l, name)])[1])
                if name == "gl0":
                    act.wait_ge(sq_added, KT * (l + 1))
                if n >= 1:
                    act.wait_ge(silu_ok, n)
                if plan.ropes[(l, name)]:
                    act.wait_ge(rot_ok, plan.ropes[(l, name)])
                act.activation(swp[:, :], e_slot((l, name)), ACT.Tanh, scale=0.5).then_inc(gate_tanh, 1)

            for t in range(1, TT, 2):
                act.dma_start(x_tok[:, t, :], x[0, t * P:(t + 1) * P, :]).then_inc(x_in, 16)
            split_hi(0)
            split_hi(1)
            split = N_RING
            act.wait_ge(a_dve, 2)
            act.wait_ge(lam_ok, 1)
            act.activation(soft[:, 2, :], soft[:, 1, :], ACT.Exp, scale=-1.0).then_inc(exp_lam, 1)
            for m in range(KT):
                act.wait_ge(z_dve, m + 1)
                norm_tile(-1, m)
            last = None

            for st in sched:
                kind = st[0]
                if kind in ("Z", "OUT") and split < len(plan.split):
                    split_hi(split)
                    split += 1
                if kind == "Z" and st[2] == "gl0":
                    rstd_in(st[1] - 1)
                if kind == "Z" and stem(st[2]) in ("gl", "gn"):
                    silu_tanh(*st[1:], plan.silus[st[1:]])
                elif kind == "GATES":
                    _, l, t = st
                    n = CT * l + t
                    if n == 0:
                        act.wait_ge(lru_par, 1)
                    else:
                        act.wait_ge(m_ok, n)
                    act.wait_ge(z_full, z_no[(*st, "a")] + 1)
                    act.activation(THR, z_bank((*st, "a"))[:, :], ACT.Tanh, bias=hba[:, n:n + 1], scale=0.5).then_inc(z_act, 1)
                    act.wait_ge(z_full, z_no[(*st, "i")] + 1)
                    act.activation(THI, z_bank((*st, "i"))[:, :], ACT.Tanh, bias=hbi[:, n:n + 1], scale=0.5).then_inc(z_act, 1)
                    act.wait_ge(z_act, plan.freed(plan.z, z_no[(*st, "i")])[1])
                    act.activation(A[t % 2], THR, ACT.Exp, bias=nsp[:, n:n + 1], scale=nsp[:, n:n + 1]).then_inc(a_ok, 1)
                    act.activation(TH, THR, ACT.Tanh, bias=psp[:, n:n + 1], scale=psp[:, n:n + 1]).then_inc(th_ok, 1)
                elif kind == "LRU":
                    _, l, half = st
                    act.wait_ge(m_ok, CT * l + 2 * half + 2)
                    for t in (2 * half, 2 * half + 1):
                        act.activation(M[t % 2], M[t % 2], ACT.Sqrt, scale=0.25).then_inc(root_m, 1)
                    for t in (2 * half, 2 * half + 1):
                        act.wait_ge(ylru_ok, CT * l + t + 1)
                        if l >= 1 and t == 0:
                            act.wait_ge(z_full, z_no[("OUT", l - 1, KT - 1)] + 1)
                        act.activation(y_hi[:, t, :], UC[t % 2], ACT.Copy).then_inc(ylru_hi, 1)
                elif kind == "SILU":
                    c = 2 * st[1] + st[2]
                    act.wait_ge(hid_in, c + 1)
                    act.activation(hid[:, :, :], hb[:, :, 0:NCOL - 1], ACT.Tanh, scale=0.5).then_inc(hid_tanh, 1)
                elif kind == "ROPE":
                    n = rope_no[st[1:]]
                    act.wait_ge(rot_ok, n + 1)
                    _, l, name = st
                    if l >= 1 and name == "ks":
                        act.wait_ge(s_full, 4 * units_before(l))
                    for g in range(N_KV):
                        own, other = slice(g * HD, (g + 1) * HD), slice((1 - g) * HD, (2 - g) * HD)
                        e = e_slot(st[1:])[own, :]
                        if stem(name) == "q":
                            ins = act.activation(q_st[own, GROUP * g + int(name[-1]), :], e, ACT.Copy)
                        else:
                            keys = k_st[:, 0 if name == "ks" else 1, g, :, :]
                            act.activation(keys[own, 0, :], e, ACT.Copy)
                            ins = act.activation(keys[other, 1, :], e, ACT.Copy)
                    ins.then_inc(rope_hi, 1)
                elif kind == "TURN":
                    _, l, name = st
                    act.wait_ge(a_full, aux_no[st] + 1)
                    if l >= 1:
                        act.wait_ge(pv_done, turns_before(l))
                    if name == "gate":
                        act.activation(gates[:, :, :], a_ps[:, 0:TT * N_GATE].rearrange("p (t n) -> p t n", t=TT),
                                       ACT.Tanh, scale=0.5).then_inc(a_act, 1)
                    else:
                        act.activation(v_sb[:, 0 if name == "vs" else 1, :, :],
                                       a_ps[:, :].rearrange("p (t n) -> p t n", t=TT), ACT.Copy).then_inc(a_act, 1)
                elif kind == "CSOFT":
                    act.wait_ge(cs_sub, st[1] + 1)
                    act.activation(sc[:, :, :, :], sc[:, :, :, :], ACT.Exp, scale=-1.0).then_inc(cs_exp, 1)
                elif kind == "UNIT":
                    _, l, unit, fill = st
                    for what, k in plan.unit_order(plan.turns_of(last) if last else 0):
                        if what == "S" and unit:
                            u, W = unit_no[(l, *unit)], P * (unit[0] + 1)
                            n = 4 * u + k
                            act.wait_ge(min_ok, n + 1)
                            if k == 0:
                                if u == units_before(l):
                                    act.wait_ge(ylru_lo, CT * (l + 1))
                                if u >= 2:
                                    act.wait_ge(t_full, first_turn[plan.units[u - 1]])
                                    act.wait_ge(p_ok, 4 * (u - 1))
                            act.activation(probs[:, 4 * (u % 2) + k, 0:W], s_ps[n % 3][:, 0:W], ACT.Exp, scale=-1.0,
                                           bias=mn[:, u % 2, k:k + 1], accum_out=rs[:, u % 2, k:k + 1]).then_inc(exp_ok, 1)
                        elif what == "T" and last:
                            n, rows = first_turn[last] + k, P if k <= last[1] else NC
                            if n % 2 == 0:
                                act.wait_ge(t_full, n + 1)
                                if n >= N_PT:
                                    act.wait_ge(pv_done, n - N_PT + 1)
                                act.activation(probsT[0:rows, n % N_PT, :], t_ps[0][0:rows, :], ACT.Copy).then_inc(pt_act, 1)
                    for name in fill:
                        split_hi(split)
                        split += 1
                        silu_tanh(l, name, plan.silus[(l, name)])
                    if last and last[2:] == (1, 1):
                        i = last[1]
                        act.wait_ge(ynsa_ok, TT * l + TT - i)
                        act.activation(y_hi[:, CT:KT, i * P:(i + 1) * P],
                                       e_slot((l, f"y{i}")).rearrange("p (r q) -> p r q", r=GROUP),
                                       ACT.Copy).then_inc(ynsa_hi, 1)
                    last = (l, *unit) if unit else None
                elif kind == "OUT":
                    _, l, m = st
                    act.wait_ge(x_new, KT * l + m + 1)
                    norm_tile(l, m)
                elif kind == "FINAL":
                    rstd_in(DEPTH - 1)
                    for m in range(KT):
                        act.wait_ge(z_full, z_no[("F", m)] + 1)
                        act.activation(x_tok[:, :, m * P:(m + 1) * P],
                                       z_bank(("F", m))[:, :].rearrange("p (t n) -> p t n", t=TT),
                                       ACT.Copy).then_inc(tok_ok, 1)

        @block.vector
        def _(dve):
            links = [0]

            def link(ins):
                links[0] += 1
                ins.then_inc(dve_link, 1)
                dve.wait_ge(dve_link, links[0])

            def h_low(tag, m):
                n = (tag + 1) * KT + m
                dve.wait_ge(h_hi_ok, n + 1)
                dve.scalar_tensor_tensor(out=h_lo[:, m, :], in0=xT[:, m, :], scalar=par[:, PG + n:PG + n + 1],
                                         in1=h_hi[:, m, :].bitcast(F32), op0=ALU.mult, op1=ALU.subtract).then_inc(h_lo_ok, 1)

            def split_lo(n):
                if plan.split[n][0] == "OUT":
                    dve.wait_ge(hi_split, n + 1)
                    dve.tensor_tensor(w_lo[:, n % N_RING, :], stage_of(plan.split[n]),
                                      w_hi[:, n % N_RING, :].bitcast(F32), ALU.subtract).then_inc(lo_dve, 1)

            def mean_square(tag):
                dve.wait_ge(a_full, aux_no[("ss", tag)] + 1)
                dve.tensor_scalar(ms[:, :], a_ps[:, 0:TT], 1.0 / D_MODEL, EPS, ALU.mult, ALU.add).then_inc(a_dve, 1)

            def diagonal(tag):
                dve.wait_ge(root_ok, tag + 2)
                for t in range(TT):
                    ins = dve.tensor_scalar(diag[:, t * P:(t + 1) * P], ident[:, :], rt[:, t:t + 1], None, ALU.mult)
                ins.then_inc(diag_ok, 1)

            def wait_e(key):
                n = e_no[key]
                if n < N_E:
                    return
                l, name = plan.e[n - N_E]
                if (l, name) in rope_no:
                    dve.wait_ge(rope_lo, rope_no[(l, name)] + 1)
                elif name in ("kc", "vc"):
                    dve.wait_ge(flat_ok, 2 * l + (name == "vc") + 1)
                elif name in ("vs", "vw", "gate"):
                    dve.wait_ge(a_full, aux_no[("TURN", l, name)] + 1)
                elif stem(name) in ("gl", "gn"):
                    dve.wait_ge(silu_ok, plan.silus[(l, name)] + 1)
                elif stem(name) == "y":
                    dve.wait_ge(ynsa_lo, TT * l + TT - int(name[-1]))

            def silu(l, name, n):
                dve.wait_ge(gate_tanh, n + 1)
                dve.scalar_tensor_tensor(out=silu_g[:, int(name[-1]), :], in0=swp[:, :], scalar=1.0,
                                         in1=e_slot((l, name)), op0=ALU.add, op1=ALU.mult).then_inc(silu_ok, 1)

            def projected(st):
                _, l, name = st
                dve.wait_ge(z_full, z_no[st] + 1)
                if stem(name) == "u":
                    dst = upad[:, CONV_W - 1:]
                    before = CT * l + int(name[-1])
                    if before >= 1:
                        dve.wait_ge(conv_ok, before)
                else:
                    wait_e((l, name))
                    dst = e_slot((l, name))
                if name == "gl0":
                    dve.wait_ge(a_act, plan.freed(plan.aux, aux_no[("rb", l - 1)])[1])
                if stem(name) == "q":
                    dve.scalar_tensor_tensor(out=dst, in0=z_bank(st)[:, :], scalar=-(HD ** -0.5), in1=rstd[:, :],
                                             op0=ALU.mult, op1=ALU.mult).then_inc(z_dve, 1)
                else:
                    dve.tensor_tensor(dst, z_bank(st)[:, :], rstd[:, :], ALU.mult).then_inc(z_dve, 1)
                dve.wait_ge(z_dve, plan.freed(plan.z, z_no[st])[1])

            dve.wait_ge(a_full, aux_no["params"] + 1)
            dve.tensor_copy(par[:, :], a_ps[:, 0:NPAR]).then_inc(a_dve, 1)
            dve.wait_ge(a_full, aux_no["pos"] + 1)
            dve.tensor_copy(posT[:, :, :, :], a_ps[:, 0:2 * DEPTH * NPAIR]
                            .rearrange("p (v l j) -> p v l j", v=2, l=DEPTH)).then_inc(a_dve, 1)
            dve.wait_ge(a_dve, 2)
            dve.tensor_scalar(hba[:, :], par[:, PBA:PBA + 8], 0.5, None, ALU.mult)
            dve.tensor_scalar(hbi[:, :], par[:, PBI:PBI + 8], 0.5, None, ALU.mult)
            lam, LG, RC, S2 = par[:, PLAM:PLAM + 8], soft[:, 0, :], soft[:, 3, :], soft[:, 4, :]
            link(dve.tensor_scalar(LG, lam, -1.0, None, ALU.mult))
            dve.tensor_tensor(soft[:, 1, :], lam, LG, ALU.max).then_inc(lam_ok, 1)
            dve.wait_ge(exp_lam, 1)
            link(dve.tensor_scalar(RC, soft[:, 2, :], 2.0, None, ALU.add))
            link(dve.reciprocal(RC, RC))
            link(dve.tensor_tensor(RC, RC, soft[:, 2, :], ALU.mult))
            link(dve.tensor_tensor(S2, RC, RC, ALU.mult))
            link(dve.tensor_scalar(soft[:, 2, :], S2, 1.0 / 19, None, ALU.mult))
            for n in (17, 15, 13, 11, 9, 7, 5, 3):
                link(dve.scalar_tensor_tensor(out=soft[:, 2, :], in0=soft[:, 2, :], scalar=1.0 / n, in1=S2,
                                              op0=ALU.add, op1=ALU.mult))
            link(dve.scalar_tensor_tensor(out=RC, in0=soft[:, 2, :], scalar=1.0, in1=RC, op0=ALU.add, op1=ALU.mult))
            link(dve.tensor_scalar(LG, LG, 0.0, None, ALU.max))
            link(dve.scalar_tensor_tensor(out=LG, in0=RC, scalar=2.0, in1=LG, op0=ALU.mult, op1=ALU.add))
            dve.tensor_scalar(nsp[:, :], LG, -4.0, None, ALU.mult)
            link(dve.tensor_scalar(psp[:, :], LG, 4.0, None, ALU.mult))
            dve.tensor_copy(soft[:, 1, :], psp[:, :]).then_inc(lru_par, 1)
            for m in range(KT):
                dve.wait_ge(z_full, z_no[("X", m)] + 1)
                dve.tensor_copy(xT[:, m, :], z_bank(("X", m))[:, :]).then_inc(z_dve, 1)
                if m >= 1:
                    h_low(-1, m - 1)
            h_low(-1, KT - 1)
            mean_square(-1)
            diagonal(-1)
            split = N_RING
            last = None

            for st in sched:
                kind = st[0]
                if kind in ("Z", "OUT") and split < len(plan.split):
                    split_lo(split)
                    split += 1
                if kind == "Z":
                    _, l, name = st
                    projected(st)
                    if stem(name) in ("gl", "gn"):
                        silu(l, name, plan.silus[(l, name)])
                    elif stem(name) == "u":
                        t = int(name[-1])
                        n = CT * l + t
                        uc = UC[t % 2]

                        def tap(j):
                            c = PCW + (CONV_W * l + j) * CT + t
                            return upad[:, j:j + SEQ], par[:, c:c + 1]
                        if t >= 2:
                            dve.wait_ge(ylru_lo, n - 1)
                        src, w = tap(0)
                        link(dve.tensor_scalar(uc, src, w, par[:, PCB + n:PCB + n + 1], ALU.mult, ALU.add))
                        for j in range(1, CONV_W):
                            src, w = tap(j)
                            ins = dve.scalar_tensor_tensor(out=uc, in0=src, scalar=w, in1=uc, op0=ALU.mult, op1=ALU.add)
                            if j < CONV_W - 1:
                                link(ins)
                        ins.then_inc(conv_ok, 1)
                elif kind == "GATES":
                    _, l, t = st
                    n = CT * l + t
                    dve.wait_ge(th_ok, n + 1)
                    dve.scalar_tensor_tensor(out=IU[t % 2], in0=THI, scalar=1.0, in1=UC[t % 2], op0=ALU.add, op1=ALU.mult)
                    dve.wait_ge(sq_ok, n + 1)
                    dve.scalar_tensor_tensor(out=M[t % 2], in0=SQ, scalar=1.0, in1=TH, op0=ALU.add, op1=ALU.mult).then_inc(m_ok, 1)
                elif kind == "LRU":
                    _, l, half = st
                    for t in (2 * half, 2 * half + 1):
                        n = CT * l + t
                        dve.wait_ge(root_m, n + 1)
                        link(dve.tensor_tensor(IU[t % 2], IU[t % 2], M[t % 2], ALU.mult))
                        link(dve.tensor_tensor_scan(UC[t % 2], A[t % 2], IU[t % 2], 0.0, ALU.mult, ALU.add))
                        dve.scalar_tensor_tensor(out=UC[t % 2], in0=UC[t % 2], scalar=0.5, in1=silu_g[:, t, :],
                                                 op0=ALU.mult, op1=ALU.mult).then_inc(ylru_ok, 1)
                elif kind == "FLAT":
                    _, l, kv = st
                    c = 2 * l + kv
                    src = e_slot((l, "kc" if kv == 0 else "vc"))
                    if c >= 1:
                        dve.wait_ge(a_full, aux_no[("C1", (c - 1) // 2, (c - 1) % 2)] + 1)
                    if kv == 0 and l >= 1:
                        dve.wait_ge(t_full, turns_before(l))
                    for g in range(N_KV):
                        tokens = src[g * HD:(g + 1) * HD, :].rearrange("p (c j h) -> p h j c", j=NPAIR // 2, h=2)
                        for h in range(2):
                            for a in range(2):
                                dve.tensor_copy(flat[h * HD:(h + 1) * HD, a * 8:a * 8 + 8, g * NC:(g + 1) * NC],
                                                tokens[:, h, :, a:a + NC])
                    dve.tensor_copy(flat[:, :, NCOL - 1:NCOL], posT[:, kv, l, :].rearrange("p (j a) -> p j a", a=1)).then_inc(flat_ok, 1)
                elif kind == "SILU":
                    _, l, kv = st
                    c = 2 * l + kv
                    dve.wait_ge(a_full, aux_no[("C1", l, kv)] + 1)
                    dve.tensor_copy(hb[:, :, :], a_ps[:, 0:HT * (NCOL + 1)].rearrange("p (m c) -> p m c", m=HT)[:, :, 0:NCOL]).then_inc(a_dve, 1)
                    dve.wait_ge(a_dve, plan.freed(plan.aux, aux_no[("C1", l, kv)])[1])
                    for m in range(HT):
                        ins = dve.tensor_scalar(hb[:, m, 0:NCOL - 1], hb[:, m, 0:NCOL - 1], hb[:, m, NCOL - 1:NCOL], None, ALU.add)
                    ins.then_inc(hid_in, 1)
                    dve.wait_ge(hid_tanh, c + 1)
                    dve.scalar_tensor_tensor(out=hid[:, :, :], in0=hid[:, :, :], scalar=1.0, in1=hb[:, :, 0:NCOL - 1],
                                             op0=ALU.add, op1=ALU.mult).then_inc(hid_ok, 1)
                elif kind == "HID":
                    _, l, kv = st
                    dve.wait_ge(a_full, aux_no[st] + 1)
                    if kv == 0:
                        dve.tensor_scalar(kc_bd[0:HD, 0:NC], a_ps[0:HD, 0:NC], 0.5, None, ALU.mult)
                        dve.tensor_scalar(kc_bd[HD:P, NC:2 * NC], a_ps[HD:P, NC:2 * NC], 0.5, None, ALU.mult).then_inc(a_dve, 1)
                    else:
                        dve.tensor_scalar(vc_sb[:, :, :], a_ps[0:NC, 0:P].rearrange("p (g d) -> p g d", g=N_KV), 0.5, None,
                                          ALU.mult).then_inc(a_dve, 1)
                elif kind == "ROPE":
                    _, l, name = st
                    n, e = rope_no[(l, name)], e_slot((l, name))
                    if stem(name) == "q":
                        r = int(name[-1])
                        dve.wait_ge(a_full, aux_no[st] + 1)
                        dve.tensor_tensor(sc[:, :, 2 * r:2 * r + 2, :],
                                          a_ps[:, 0:TT * N_KV * NC].rearrange("p (i g c) -> p i g c", i=TT, g=N_KV),
                                          mask_c[:, :, :].rearrange("p i (a c) -> p i a c", a=1).to_broadcast([P, TT, N_KV, NC]),
                                          ALU.add).then_inc(a_dve, 1)
                    if n >= 1:
                        dve.wait_ge(rot_ok, n)
                    dve.wait_ge(silu_ok, plan.silus[st])
                    dve.wait_ge(tab_in, 32)
                    for a in range(4):
                        src = slice(32 * (a ^ 1), 32 * (a ^ 1) + 32)
                        ins = dve.tensor_tensor(swp[32 * a:32 * a + 32, :], e[src, :], sinT[src, :], ALU.mult)
                    link(ins)
                    link(dve.tensor_tensor(e, e, cosT[:, :], ALU.mult))
                    dve.tensor_tensor(e, e, swp[:, :], ALU.add).then_inc(rot_ok, 1)
                elif kind == "LOW":
                    _, l, name = st
                    n, e = rope_no[(l, name)], e_slot((l, name))
                    dve.wait_ge(rope_hi, n + 1)
                    for g in range(N_KV):
                        own, other = slice(g * HD, (g + 1) * HD), slice((1 - g) * HD, (2 - g) * HD)
                        if stem(name) == "q":
                            q = q_st[:, GROUP * g + int(name[-1]), :]
                            ins = dve.tensor_tensor(q[other, :], e[own, :], q[own, :].bitcast(F32), ALU.subtract)
                        else:
                            keys = k_st[:, 0 if name == "ks" else 1, g, :, :]
                            hi = keys[own, 0, :].bitcast(F32)
                            dve.tensor_tensor(keys[other, 0, :], e[own, :], hi, ALU.subtract)
                            ins = dve.tensor_tensor(keys[own, 1, :], e[own, :], hi, ALU.subtract)
                    ins.then_inc(rope_lo, 1)
                elif kind == "TURN" and st[2] == "gate":
                    dve.wait_ge(a_act, plan.freed(plan.aux, aux_no[st])[1])
                    link(dve.tensor_scalar(gates[:, :, :], gates[:, :, :], 1.0, 0.5, ALU.add, ALU.mult))
                elif kind == "CSOFT":
                    l = st[1]
                    dve.wait_ge(a_dve, plan.freed(plan.aux, aux_no[("ROPE", l, "q3")])[1])
                    link(dve.tensor_reduce(mnc[:, :, :], sc[:, :, :, :], AX.X, ALU.min))
                    sc3 = sc[:, :, :, :].rearrange("p i h c -> p (i h) c")

                    def spread(v):
                        return v[:, :, :].rearrange("p i (h a) -> p (i h) a", a=1).to_broadcast([P, TT * 8, NC])
                    dve.tensor_tensor(sc3, sc3, spread(mnc), ALU.subtract).then_inc(cs_sub, 1)
                    dve.wait_ge(cs_exp, l + 1)
                    link(dve.tensor_reduce(rsc[:, :, :], sc[:, :, :, :], AX.X, ALU.add))
                    link(dve.reciprocal(rsc[:, :, :], rsc[:, :, :]))
                    gate0 = gates[:, :, :].rearrange("p i (g r b) -> p i b r g", g=N_KV, b=3)[:, :, 0, :, :]
                    r4 = rsc[:, :, :].rearrange("p i (r g) -> p i r g", g=N_KV)
                    link(dve.tensor_tensor(r4, r4, gate0, ALU.mult))
                    link(dve.tensor_tensor(rsc[:, :, :], rsc[:, :, :],
                                           row_ok[:, :].rearrange("p (i a) -> p i a", a=1).to_broadcast([P, TT, 8]), ALU.mult))
                    dve.tensor_tensor(sc3, sc3, spread(rsc), ALU.mult).then_inc(cs_ok, 1)
                elif kind == "UNIT":
                    _, l, unit, fill = st
                    for what, k in plan.unit_order(plan.turns_of(last) if last else 0):
                        if what == "S" and unit:
                            u, W = unit_no[(l, *unit)], P * (unit[0] + 1)
                            n = 4 * u + k
                            dve.wait_ge(s_full, n + 1)
                            if k == 0 and u >= 2:
                                dve.wait_ge(exp_ok, 4 * (u - 1))
                            dve.tensor_reduce(mn[:, u % 2, k:k + 1], s_ps[n % 3][:, 0:W], AX.X, ALU.min).then_inc(min_ok, 1)
                        elif what == "T" and last:
                            n, rows = first_turn[last] + k, P if k <= last[1] else NC
                            if n % 2 == 1:
                                dve.wait_ge(t_full, n + 1)
                                if n >= N_PT:
                                    dve.wait_ge(pv_done, n - N_PT + 1)
                                dve.tensor_copy(probsT[0:rows, n % N_PT, :], t_ps[1][0:rows, :]).then_inc(pt_dve, 1)
                    if unit:
                        i, b, pair = unit
                        c = coef[:, u % 2, :]
                        dve.wait_ge(exp_ok, 4 * (u + 1))
                        if u >= 2:
                            dve.wait_ge(p_ok, 4 * (u - 1))
                        link(dve.reciprocal(c, rs[:, u % 2, :]))
                        gate = gates[:, i, :].rearrange("p (g r b) -> p b g r", g=N_KV, b=3)[:, 1 + b, :, 2 * pair:2 * pair + 2]
                        c4 = c.rearrange("p (g r) -> p g r", g=N_KV)
                        link(dve.tensor_tensor(c4, c4, gate, ALU.mult))
                        for j in range(4):
                            ph = probs[:, 4 * (u % 2) + j, 0:W]
                            dve.tensor_scalar(ph, ph, c[:, j:j + 1], None, ALU.mult).then_inc(p_ok, 1)
                    for name in fill:
                        split_lo(split)
                        split += 1
                        projected(("Z", l, name))
                        silu(l, name, plan.silus[(l, name)])
                    if last and last[2:] == (1, 1):
                        i = last[1]
                        n = TT * l + TT - 1 - i
                        key = (l, f"y{i}")
                        e = e_slot(key).rearrange("p (r q) -> p r q", r=GROUP)
                        dve.wait_ge(pv_done, first_turn[last] + plan.turns_of(last))
                        wait_e(key)
                        dve.scalar_tensor_tensor(out=e, in0=o_ps[:, :].rearrange("p (r q) -> p r q", r=GROUP), scalar=0.5,
                                                 in1=silu_g[:, :, i * P:(i + 1) * P], op0=ALU.mult, op1=ALU.mult).then_inc(ynsa_ok, 1)
                        dve.wait_ge(ynsa_hi, n + 1)
                        dve.tensor_tensor(y_lo[:, CT:KT, i * P:(i + 1) * P], e,
                                          y_hi[:, CT:KT, i * P:(i + 1) * P].bitcast(F32), ALU.subtract).then_inc(ynsa_lo, 1)
                    last = (l, *unit) if unit else None
                elif kind == "OUT":
                    _, l, m = st
                    dve.wait_ge(z_full, z_no[st] + 1)
                    dve.tensor_tensor(xT[:, m, :], xT[:, m, :], z_bank(st)[:, :], ALU.add).then_inc(x_new, 1)
                    if l + 1 < DEPTH:
                        h_low(l, m)
                elif kind == "NORM":
                    mean_square(st[1])
                    diagonal(st[1])
                elif kind == "FINAL":
                    dve.wait_ge(a_act, plan.freed(plan.aux, aux_no[("rb", DEPTH - 1)])[1])
                    for m in range(KT):
                        dve.scalar_tensor_tensor(out=xT[:, m, :], in0=xT[:, m, :], scalar=par[:, PFG + m:PFG + m + 1],
                                                 in1=rstd[:, :], op0=ALU.mult, op1=ALU.mult).then_inc(fin_ok, 1)

        @block.tensor
        def _(pe):
            def z_product(key, first, last):
                n = split_no[key]
                slot, bank = n % N_RING, z_bank(key)
                l, is_out = key[1], key[0] == "OUT"
                x_hi, x_lo = (y_hi, y_lo) if is_out else (h_hi, h_lo)
                if first == 0:
                    pe.wait_ge(hi_split, n + 1)
                    wait_low(pe, n)
                    wait_z(pe, key)
                for at in range(first, last):
                    k, part = divmod(at, 3)
                    if part == 0 and not is_out and key[2] == "gl0":
                        pe.wait_ge(h_lo_ok, KT * l + k + 1)
                    w = (w_hi, w_hi, w_lo)[part]
                    act_in = (x_hi, x_lo, x_hi)[part]
                    ins = pe.matmul(bank[:, :], w[:, slot, k * P:(k + 1) * P], act_in[:, k, :],
                                    start=(at == 0), stop=(at == 3 * KT - 1))
                if last == 3 * KT:
                    ins.then_inc(z_full, 1)

            def sum_squares(tag):
                wait_aux(pe, ("ss", tag))
                pe.wait_ge(sq_added, KT * (tag + 2))
                for t in range(TT):
                    ins = pe.matmul(a_ps[:, t:t + 1], sq_acc[:, t * P:(t + 1) * P], ones[:, 0:1], start=True, stop=True)
                ins.then_inc(a_full, 1)

            def spread_rstd(tag):
                wait_aux(pe, ("rb", tag))
                pe.wait_ge(diag_ok, tag + 2)
                pe.matmul(a_ps[:, :], ones[:, :], diag, start=True, stop=True).then_inc(a_full, 1)

            def scores(u, j):
                l, i, b, _ = plan.units[u]
                h = head(plan.units[u], j)
                n, W, g = 4 * u + j, P * (i + 1), h // GROUP
                if n >= 3:
                    pe.wait_ge(exp_ok, n - 2)
                q = q_st[:, h, i * P:(i + 1) * P]
                bank = s_ps[n % 3]
                pe.matmul(bank[:, 0:W], q, k_st[:, b, g, 0, 0:W], start=True, stop=False)
                pe.matmul(bank[:, W - P:W], ident_b[:, :], causal_b[:, :], start=False, stop=False)
                pe.matmul(bank[:, 0:W], q, k_st[:, b, g, 1, 0:W], start=False, stop=True).then_inc(s_full, 1)

            def turn(key, k):
                l, i, b, pair = key
                u, n = unit_no[key], first_turn[key] + k
                bank = t_ps[n % 2]
                if n >= 2:
                    wait_turned(pe, n - 2)
                if k == 0:
                    pe.wait_ge(p_ok, 4 * (u + 1))
                if k > i:
                    pe.wait_ge(cs_ok, l + 1)
                for j in range(4):
                    if k <= i:
                        ins = pe.transpose(bank[:, j * P:(j + 1) * P], probs[:, 4 * (u % 2) + j, k * P:(k + 1) * P], ident[:, :])
                    else:
                        g, r = divmod(head(key, j), GROUP)
                        ins = pe.transpose(bank[0:NC, j * P:(j + 1) * P], sc[:, i, 2 * r + g, :], ident[:, :])
                ins.then_inc(t_full, 1)

            def weigh(key, k):
                l, i, b, pair = key
                n = first_turn[key] + k
                wait_turned(pe, n)
                first = b == 0 and k == 0 and pair == 0
                done = TT * l + TT - 1 - i
                if first and done >= 1:
                    pe.wait_ge(ynsa_ok, done)
                for g in range(N_KV):
                    if k <= i:
                        v, rows = v_sb[:, b, k, g * HD:(g + 1) * HD], P
                    else:
                        v, rows = vc_sb[:, g, :], NC
                    ins = pe.matmul(o_ps[g * HD:(g + 1) * HD, pair * 2 * P:(pair + 1) * 2 * P], v,
                                    probsT[0:rows, n % N_PT, g * 2 * P:(g + 1) * 2 * P],
                                    start=first, stop=(k > i), skip_group_check=True)
                ins.then_inc(pv_done, 1)

            pe.wait_ge(first_consts, 1)
            pe.wait_ge(par_in, 16 * 9)
            pe.transpose(a_ps[:, 0:NPAR], par_row[0:NPAR, :], ident[0:NPAR, 0:NPAR]).then_inc(a_full, 1)
            wait_aux(pe, "pos")
            n_pos = 2 * DEPTH * NPAIR
            pe.transpose(a_ps[:, 0:n_pos], pos_row[0:n_pos, :], ident[0:n_pos, 0:n_pos]).then_inc(a_full, 1)
            pe.wait_ge(x_in, 16 * TT)
            for m in range(KT):
                wait_z(pe, ("X", m))
                for t in range(TT):
                    ins = pe.transpose(z_bank(("X", m))[:, t * P:(t + 1) * P], x_tok[:, t, m * P:(m + 1) * P], ident[:, :])
                ins.then_inc(z_full, 1)

            last = None
            for st in sched:
                kind = st[0]
                if kind in ("Z", "OUT"):
                    if kind == "OUT" and st[2] == 0:
                        pe.wait_ge(ylru_lo, CT * (st[1] + 1))
                        pe.wait_ge(ynsa_lo, TT * (st[1] + 1))
                    z_product(st, 0, 3 * KT)
                    if kind == "Z" and st[2] == "gl0":
                        sum_squares(st[1] - 1)
                    if kind == "Z" and st[2] == "gl1":
                        spread_rstd(st[1] - 1)
                elif kind == "NORM" and st[1] == DEPTH - 1:
                    sum_squares(st[1])
                    spread_rstd(st[1])
                elif kind == "GATES":
                    _, l, t = st
                    pe.wait_ge(conv_ok, CT * l + t + 1)
                    if t == 0:
                        pe.wait_ge(small_in, 96 * (l + 1))
                    for ab, which in enumerate("ai"):
                        wait_z(pe, (*st, which))
                        pe.matmul(z_bank((*st, which))[:, :], bd[:, t, ab, :], UC[t % 2], start=True, stop=True).then_inc(z_full, 1)
                elif kind == "C1":
                    _, l, kv, part = st
                    if part == 0:
                        wait_aux(pe, ("C1", l, kv))
                        pe.wait_ge(flat_ok, 2 * l + kv + 1)
                    pe.wait_ge(staged[load_no[st] % N_STAGE], plan.staged_at[st])
                    w1 = stage_of(st).rearrange("p (j n) -> p j n", j=4)
                    for j in range(4):
                        for m in range(HT):
                            ins = pe.matmul(a_ps[:, m * (NCOL + 1):m * (NCOL + 1) + NCOL], w1[:, j, m * P:(m + 1) * P],
                                            flat[:, 4 * part + j, :], start=(part == j == m == 0),
                                            stop=(part == 3 and j == 3), skip_group_check=True)
                    ins.then_inc(a_full if part == 3 else cmp_used, 1)
                elif kind == "HID":
                    _, l, kv = st
                    wait_aux(pe, st)
                    pe.wait_ge(small_in, 96 * (l + 1))
                    pe.wait_ge(hid_ok, 2 * l + kv + 1)
                    for g in range(N_KV):
                        for m in range(HT):
                            h = hid[:, m, g * NC:(g + 1) * NC]
                            if kv == 0:
                                o, a, b = a_ps[g * HD:(g + 1) * HD, g * NC:(g + 1) * NC], w2[:, kv, m, :], h
                            else:
                                o, a, b = a_ps[0:NC, g * HD:(g + 1) * HD], h, w2[:, kv, m, :]
                            ins = pe.matmul(o, a, b, start=(m == 0), stop=(m == HT - 1), skip_group_check=True)
                    ins.then_inc(a_full, 1)
                elif kind == "TURN":
                    _, l, name = st
                    who, count = plan.freed(plan.z, z_no[("Z", l, name)])
                    pe.wait_ge(z_free[who], count)
                    wait_aux(pe, st)
                    e = e_slot((l, name))
                    rows = N_GATE if name == "gate" else P
                    for t in range(TT):
                        ins = pe.transpose(a_ps[:, t * rows:(t + 1) * rows], e[0:rows, t * P:(t + 1) * P], ident[0:rows, 0:rows])
                    ins.then_inc(a_full, 1)
                elif kind == "ROPE" and stem(st[2]) == "q":
                    _, l, name = st
                    who, count = plan.freed(plan.z, z_no[("Z", l, name)])
                    pe.wait_ge(z_free[who], count)
                    wait_aux(pe, st)
                    for i in range(TT):
                        ins = pe.matmul(a_ps[:, i * N_KV * NC:(i + 1) * N_KV * NC], e_slot((l, name))[:, i * P:(i + 1) * P],
                                        kc_bd[:, :], start=True, stop=True)
                    ins.then_inc(a_full, 1)
                elif kind == "UNIT":
                    _, l, unit, fill = st
                    if unit and unit_no[(l, *unit)] == units_before(l):
                        pe.wait_ge(consts, N_CONST)
                        pe.wait_ge(a_dve, plan.freed(plan.aux, aux_no[("ROPE", l, "q3")])[1])
                        pe.wait_ge(rope_hi, 6 * (l + 1))
                        pe.wait_ge(rope_lo, 6 * (l + 1))
                    for what, k in plan.unit_order(plan.turns_of(last) if last else 0):
                        if what == "S" and unit:
                            scores(unit_no[(l, *unit)], k)
                            if k >= 1:
                                for name in fill:
                                    z_product(("Z", l, name), (k - 1) * KT, k * KT)
                        elif what == "T" and last:
                            turn(last, k)
                        elif what == "W" and last:
                            weigh(last, k)
                    last = (l, *unit) if unit else None
                elif kind == "FINAL":
                    for m in range(KT):
                        wait_z(pe, ("F", m))
                        pe.wait_ge(fin_ok, m + 1)
                        for t in range(TT):
                            ins = pe.transpose(z_bank(("F", m))[:, t * P:(t + 1) * P], xT[:, m, t * P:(t + 1) * P], ident[:, :])
                        ins.then_inc(z_full, 1)


_INS = ["x", "norm_g", "w_in", "conv_w", "conv_b", "lru_wa", "lru_ba", "lru_wi", "lru_bi", "lru_lambda",
        "cmp_pos_k", "cmp_pos_v", "cmp_k_w1", "cmp_k_w2", "cmp_v_w1", "cmp_v_w2", "w_out", "final_g"]


def rope_tables():
    inv = np.float32(1.0) / np.float32(10000.0) ** (np.arange(0, HD, 2, dtype=np.float32) / np.float32(HD))
    ang = (np.arange(SEQ, dtype=np.float32)[:, None] * inv[None, :].astype(np.float32)).astype(np.float32)
    c, s = np.cos(ang).T.astype(np.float32), np.sin(ang).T.astype(np.float32)
    return np.ascontiguousarray(np.concatenate([c] * 4)), np.ascontiguousarray(np.concatenate([s, -s] * 2))


def kernel(**inputs):
    import concourse.bacc as bacc
    from concourse.bass_utils import run_bass_kernel_spmd

    nc = bacc.Bacc("TRN2", target_bir_lowering=False, num_devices=1)
    arrays, args = {}, []
    named = [(name, np.ascontiguousarray(inputs[name])) for name in _INS]
    for name, a in [*named, *zip(("rope_cos", "rope_sin"), rope_tables())]:
        arrays[f"in_{name}"] = a
        args.append(nc.dram_tensor(f"in_{name}", a.shape, mybir.dt.from_np(a.dtype), kind="ExternalInput").ap())
    args.append(nc.dram_tensor("out", (1, SEQ, D_MODEL), F32, kind="ExternalOutput").ap())
    hybrid_trunk(nc, *args)
    return run_bass_kernel_spmd(nc, [arrays], core_ids=[0]).results[0]["out"]
```
